# Optimizing a Trainium2 kernel written in Bass

```python
import math
import jax, jax.numpy as jnp
from jax import lax
import numpy as np

D_MODEL = 1024
BATCH = 1
SEQ = 256
DEPTH = 4

HEAD_DIM = 128
N_HEADS = D_MODEL // HEAD_DIM
N_DIFF_HEADS = D_MODEL // (2 * HEAD_DIM)
D_FF = 2816
ROPE_THETA = 500000.0
ROT_DIM = HEAD_DIM // 4
Q_BLOCK = 128
N_MIXERS = 3
EPS = 1e-6
NEG = -1e30
SB_NEG = -1e4
N_SB = (DEPTH + 2) // 3
N_DIFF = (DEPTH + 1) // 3
N_FOX = DEPTH // 3

kernel_name = "hybrid_sb_diff_fox_macaron"

F32 = jnp.float32

def rms_norm(x, g):
    xf = x.astype(F32)
    y = xf * lax.rsqrt(jnp.mean(xf * xf, axis=-1, keepdims=True) + EPS)
    return (y * g.astype(F32)).astype(x.dtype)

def swiglu(x, w_gate, w_up, w_down):
    return (jax.nn.silu(x @ w_gate) * (x @ w_up)) @ w_down

def partial_rope(x, pos):
    half = ROT_DIM // 2
    inv = ROPE_THETA ** (-jnp.arange(half, dtype=F32) * 2.0 / ROT_DIM)
    ang = pos.astype(F32)[:, None] * inv[None, :]
    cos = jnp.cos(ang)[None, :, None, :]
    sin = jnp.sin(ang)[None, :, None, :]
    xr = x[..., :ROT_DIM].astype(F32)
    x1, x2 = xr[..., :half], xr[..., half:]
    rot = jnp.concatenate([x1 * cos - x2 * sin, x2 * cos + x1 * sin], axis=-1).astype(x.dtype)
    return jnp.concatenate([rot, x[..., ROT_DIM:]], axis=-1)

def to_heads(t, n_heads):
    B, S, W = t.shape
    return t.reshape(B, S, n_heads, W // n_heads).transpose(0, 2, 1, 3)

def from_heads(t):
    B, H, S, d = t.shape
    return t.transpose(0, 2, 1, 3).reshape(B, S, H * d)

def block_mask(i, n_keys, strict):
    qpos = i * Q_BLOCK + jnp.arange(Q_BLOCK)
    kpos = jnp.arange(n_keys)
    if strict:
        return kpos[None, :] < qpos[:, None]
    return kpos[None, :] <= qpos[:, None]

def rev_excl_cumsum(a, n_kb):
    a4 = a.reshape(*a.shape[:-1], n_kb, Q_BLOCK)
    ar = jnp.arange(Q_BLOCK)
    upper = (ar[None, :] > ar[:, None]).astype(F32)
    within = jnp.einsum('...nc,dc->...nd', a4, upper)
    br = jnp.arange(n_kb)
    upper_b = (br[None, :] > br[:, None]).astype(F32)
    later_blocks = jnp.einsum('...n,mn->...m', jnp.sum(a4, axis=-1), upper_b)
    return (within + later_blocks[..., None]).reshape(a.shape)

def stick_breaking_attention(q, k, v):
    S = q.shape[2]
    scale = HEAD_DIM ** -0.5
    outs = []
    for i in range(S // Q_BLOCK):
        n_keys = (i + 1) * Q_BLOCK
        qb = q[:, :, i * Q_BLOCK:n_keys]
        z = jnp.einsum('bhqd,bhkd->bhqk', qb, k[:, :, :n_keys], preferred_element_type=F32) * scale
        z = jnp.where(block_mask(i, n_keys, strict=True), z, SB_NEG)
        log_one_minus = jax.nn.log_sigmoid(-z)
        w = jnp.exp(z + log_one_minus + rev_excl_cumsum(log_one_minus, i + 1))
        outs.append(jnp.einsum('bhqk,bhkd->bhqd', w.astype(v.dtype), v[:, :, :n_keys]))
    return jnp.concatenate(outs, axis=2)

def differential_attention(q, k, v, lam):
    B, H2, S, _ = q.shape
    Hd = H2 // 2
    scale = HEAD_DIM ** -0.5
    outs = []
    for i in range(S // Q_BLOCK):
        n_keys = (i + 1) * Q_BLOCK
        qb = q[:, :, i * Q_BLOCK:n_keys]
        s = jnp.einsum('bhqd,bhkd->bhqk', qb, k[:, :, :n_keys], preferred_element_type=F32) * scale
        s = jnp.where(block_mask(i, n_keys, strict=False), s, NEG)
        p = jax.nn.softmax(s, axis=-1).reshape(B, Hd, 2, Q_BLOCK, n_keys)
        a = p[:, :, 0] - lam * p[:, :, 1]
        outs.append(jnp.einsum('bhqk,bhkd->bhqd', a.astype(v.dtype), v[:, :, :n_keys]))
    return jnp.concatenate(outs, axis=2)

def forgetting_attention(q, k, v, log_f):
    S = q.shape[2]
    scale = HEAD_DIM ** -0.5
    c = jnp.cumsum(log_f.astype(F32), axis=-1)
    outs = []
    for i in range(S // Q_BLOCK):
        n_keys = (i + 1) * Q_BLOCK
        qb = q[:, :, i * Q_BLOCK:n_keys]
        s = jnp.einsum('bhqd,bhkd->bhqk', qb, k[:, :, :n_keys], preferred_element_type=F32) * scale
        s = s + c[:, :, i * Q_BLOCK:n_keys, None] - c[:, :, None, :n_keys]
        s = jnp.where(block_mask(i, n_keys, strict=False), s, NEG)
        p = jax.nn.softmax(s, axis=-1)
        outs.append(jnp.einsum('bhqk,bhkd->bhqd', p.astype(v.dtype), v[:, :, :n_keys]))
    return jnp.concatenate(outs, axis=2)

def setup_inputs(seed: int = 0) -> dict:
    key = jax.random.key(seed)
    ks = jax.random.split(key, 13)
    D, F = D_MODEL, D_FF
    x = jax.random.normal(ks[0], (BATCH, SEQ, D), F32)
    norm_g = 1.0 + 0.02 * jax.random.normal(ks[1], (DEPTH, 3, D), F32)
    final_g = 1.0 + 0.02 * jax.random.normal(ks[2], (D,), F32)
    ffn_w_gate = jax.random.normal(ks[3], (DEPTH, 2, D, F), F32) * D ** -0.5
    ffn_w_up = jax.random.normal(ks[4], (DEPTH, 2, D, F), F32) * D ** -0.5
    ffn_w_down = jax.random.normal(ks[5], (DEPTH, 2, F, D), F32) * F ** -0.5
    w_qkv = jax.random.normal(ks[6], (DEPTH, D, 3 * D), F32) * D ** -0.5
    w_o = jax.random.normal(ks[7], (DEPTH, D, D), F32) * D ** -0.5
    diff_lambda = 0.1 * jax.random.normal(ks[8], (N_DIFF, 4, HEAD_DIM), F32)
    diff_subln_g = 1.0 + 0.02 * jax.random.normal(ks[9], (N_DIFF, 2 * HEAD_DIM), F32)
    fox_w_f = jax.random.normal(ks[10], (N_FOX, D, N_HEADS), F32) * 0.5 * D ** -0.5
    fox_b_f = 2.0 + 0.1 * jax.random.normal(ks[11], (N_FOX, N_HEADS), F32)
    return {"x": x, "norm_g": norm_g, "final_g": final_g,
            "ffn_w_gate": ffn_w_gate, "ffn_w_up": ffn_w_up, "ffn_w_down": ffn_w_down,
            "w_qkv": w_qkv, "w_o": w_o,
            "diff_lambda": diff_lambda, "diff_subln_g": diff_subln_g,
            "fox_w_f": fox_w_f, "fox_b_f": fox_b_f}

def reference(x, norm_g, final_g, ffn_w_gate, ffn_w_up, ffn_w_down, w_qkv, w_o,
              diff_lambda, diff_subln_g, fox_w_f, fox_b_f):
    S = x.shape[1]
    pos = jnp.arange(S)
    for i in range(DEPTH):
        kind = i % N_MIXERS
        j = i // N_MIXERS
        x = x + 0.5 * swiglu(rms_norm(x, norm_g[i, 0]), ffn_w_gate[i, 0], ffn_w_up[i, 0], ffn_w_down[i, 0])
        h = rms_norm(x, norm_g[i, 1])
        q, k, v = jnp.split(h @ w_qkv[i], 3, axis=-1)
        if kind == 0:
            mix = from_heads(stick_breaking_attention(
                to_heads(q, N_HEADS), to_heads(k, N_HEADS), to_heads(v, N_HEADS)))
        elif kind == 1:
            B_, S_, _ = q.shape
            qh = partial_rope(q.reshape(B_, S_, 2 * N_DIFF_HEADS, HEAD_DIM), pos).transpose(0, 2, 1, 3)
            kh = partial_rope(k.reshape(B_, S_, 2 * N_DIFF_HEADS, HEAD_DIM), pos).transpose(0, 2, 1, 3)
            vh = to_heads(v, N_DIFF_HEADS)
            lam_init = 0.8 - 0.6 * math.exp(-0.3 * i)
            lp = diff_lambda[j].astype(F32)
            lam = jnp.exp(jnp.sum(lp[0] * lp[1])) - jnp.exp(jnp.sum(lp[2] * lp[3])) + lam_init
            o = differential_attention(qh, kh, vh, lam)
            o = rms_norm(o, diff_subln_g[j]) * (1.0 - lam_init)
            mix = from_heads(o)
        else:
            log_f = jax.nn.log_sigmoid((h @ fox_w_f[j] + fox_b_f[j]).astype(F32))
            mix = from_heads(forgetting_attention(
                to_heads(q, N_HEADS), to_heads(k, N_HEADS), to_heads(v, N_HEADS),
                log_f.transpose(0, 2, 1)))
        x = x + mix @ w_o[i]
        x = x + 0.5 * swiglu(rms_norm(x, norm_g[i, 2]), ffn_w_gate[i, 1], ffn_w_up[i, 1], ffn_w_down[i, 1])
    return rms_norm(x, final_g)


_drawn_inputs = setup_inputs


def setup_inputs(seed=0):
    import zlib

    import numpy as np

    out = dict(_drawn_inputs(seed))
    spreads = {}
    factors = {'final_g': 7.805, 'diff_subln_g': 14.876, 'fox_b_f': 31.064, 'fox_w_f': 8.0}
    for name, (base, spread) in spreads.items():
        noise = np.random.default_rng([zlib.crc32(name.encode()), seed]).standard_normal(out[name].shape)
        drawn = base * np.exp(spread * noise) if base else spread * noise
        out[name] = __import__('jax').numpy.asarray(drawn.astype(out[name].dtype))
    for name, factor in factors.items():
        out[name] = (out[name] * factor).astype(out[name].dtype)
    return out
```

```python
import math
from contextlib import ExitStack

import numpy as np

import concourse.bass as bass
from concourse import mybir

F32 = mybir.dt.float32
F32R = mybir.dt.float32r
ALU = mybir.AluOpType
ACT = mybir.ActivationFunctionType
AX_X = mybir.AxisListType.X

P = 128
D, T, FF, DEPTH = 1024, 256, 2816, 4
HD = 128
DT = D // P
TB = T // P
COLS = 256
CHUNK = DT * COLS
UNITS = FF // COLS
PAIRS = D // COLS
FFN_CHUNKS = 3 * UNITS
ATT_CHUNKS = 4 * PAIRS
CHUNKS = DEPTH * (2 * FFN_CHUNKS + ATT_CHUNKS)
FFN_TILES = 2 * UNITS
NORMS = 3 * DEPTH + 1
RAW = 3
RING = 6
SCALE = HD ** -0.5
EPS = 1e-6
NEG = -1e30
TRI = T + P
STICK, DIFF, FOX = range(3)
KINDS = [i % 3 for i in range(DEPTH)]
ROT = 32
LAM_INIT = 0.8 - 0.6 * math.exp(-0.3 * KINDS.index(DIFF))

C_ONES, C_IDENT, C_LATER, C_CUM = 0, 128, 256, 384
C_STRICT_T, C_CAUSAL, C_COS, C_SIN, C_ROT = 640, 1024, 1408, 1664, 1920
C_END = 1952


def constants():
    c = np.zeros((P, C_END), np.float32)
    a = np.arange(P)
    c[:, C_ONES:C_ONES + P] = 1.0
    c[:, C_IDENT:C_IDENT + P] = np.eye(P)
    c[:, C_LATER:C_LATER + P] = a[:, None] >= a[None, :]
    c[:, C_CUM:C_CUM + P] = a[:, None] <= a[None, :]
    c[:, C_CUM + P:C_CUM + 2 * P] = 1.0
    strict = np.where(a[:, None] < a[None, :], 0.0, NEG)
    causal = np.where(a[None, :] <= a[:, None], 0.0, NEG)
    for at, mask in ((C_STRICT_T, strict), (C_CAUSAL, causal)):
        c[:, at:at + P] = mask
        c[:, at + 2 * P:at + 3 * P] = mask
    half = ROT // 2
    inv = np.float32(500000.0) ** (-np.arange(half, dtype=np.float32) * np.float32(2.0) / np.float32(ROT))
    ang = (np.arange(T, dtype=np.float32)[:, None] * inv[None, :].astype(np.float32)).astype(np.float64).T
    for at, f in ((C_COS, np.cos), (C_SIN, np.sin)):
        c[0:half, at:at + T] = f(ang)
        c[half:ROT, at:at + T] = f(ang)
    for m in range(half):
        c[m + half, C_ROT + m] = -1.0
        c[m, C_ROT + m + half] = 1.0
    return c


def phases():
    out, chunk, ffn = [], 0, 0
    for layer in range(DEPTH):
        for part in range(3):
            att = part == 1
            out.append((layer, 3 * layer + part, chunk, att, layer if att else ffn))
            chunk += ATT_CHUNKS if att else FFN_CHUNKS
            ffn += not att
    return out


def trunk(nc, stream, x_in, gains, consts, lam_in, subln_in, wf_in, bf_in, out):
    with ExitStack() as ctx:
        def sb(name, shape, dt=F32):
            return ctx.enter_context(nc.sbuf_tensor(name, shape, dt))

        def sem(name):
            return ctx.enter_context(nc.semaphore(name))

        raw = sb("raw", [P, RAW, CHUNK])
        w_hi = sb("w_hi", [P, RING, CHUNK], F32R)
        w_lo = sb("w_lo", [P, RING, CHUNK], F32R)
        x = sb("x", [P, DT, T])
        xg_hi = sb("xg_hi", [P, DT, T], F32R)
        xg_lo = sb("xg_lo", [P, DT, T], F32R)
        m_hi = sb("m_hi", [P, 4, T], F32R)
        m_lo = sb("m_lo", [P, 4, T], F32R)
        scratch = sb("scratch", [P, 4, 2 * TRI])
        wide = sb("wide", [P, DT, TRI])
        v = sb("v", [P, TB, D])
        q_t = sb("q_t", [P, 2, T])
        k_t = sb("k_t", [P, 2, T])
        w_t = sb("w_t", [P, 2, TRI])
        cst = sb("cst", [P, C_END])
        gain = sb("gain", [P, NORMS, DT])
        r_row = sb("r_row", [P, T])
        r_diag = sb("r_diag", [P, T])
        mean = sb("mean", [P, TB])
        r_col = sb("r_col", [P, TB])
        half_neg = sb("half_neg", [P, TB])
        row_max = sb("row_max", [P, 2, TB])
        neg_max = sb("neg_max", [P, 2, TB])
        row_sum = sb("row_sum", [P, 2, TB])
        row_inv = sb("row_inv", [P, 2, TB])
        lam_q = sb("lam_q", [P, 4])
        lam_p = sb("lam_p", [P, 2])
        lam_e = sb("lam_e", [P, 2])
        lam = sb("lam", [P, 2])
        subln = sb("subln", [P, 2])
        subln_s = sb("subln_s", [P, 2])
        wf = sb("wf", [P, DT, 8])
        bf = sb("bf", [P, 8])
        fg = sb("fg", [P, 4, TB, 8])
        cum_col = sb("cum_col", [P, TB, 8])

        acc = ctx.enter_context(nc.psum_tensor("acc", [P, 4, 512], F32))
        work = ctx.enter_context(nc.psum_tensor("work", [P, 4, 512], F32))

        raw_loaded = [sem(f"raw_loaded{i}") for i in range(RAW)]
        const_loaded, x_loaded = sem("const_loaded"), sem("x_loaded")
        hi_ready = sem("hi_ready")
        lo_ready = sem("lo_ready")
        gate_used = sem("gate_used")
        acc_ready = sem("acc_ready")
        x_updated = sem("x_updated")
        xg_hi_ready, xg_ready = sem("xg_hi_ready"), sem("xg_ready")
        squares_ready, square_sum_ready = sem("squares_ready"), sem("square_sum_ready")
        var_ready, mean_ready, r_col_ready = sem("var_ready"), sem("mean_ready"), sem("r_col_ready")
        r_diag_ready, r_row_psum, r_row_ready = sem("r_diag_ready"), sem("r_row_psum"), sem("r_row_ready")
        gu_psum = sem("gu_psum")
        gu_scaled = sem("gu_scaled")
        silu_ready, h_ready, h_hi_ready, h_split = sem("silu_ready"), sem("h_ready"), sem("h_hi_ready"), sem("h_split")
        down_used = sem("down_used")
        out_used = sem("out_used")
        v_psum, v_ready = sem("v_psum"), sem("v_ready")
        qk_psum, qk_ready = sem("qk_psum"), sem("qk_ready")
        rope_in, rope_psum = sem("rope_in"), sem("rope_psum")
        scores_psum = sem("scores_psum")
        scores_ready = sem("scores_ready")
        exp_ready = sem("exp_ready")
        mix_in = sem("mix_in")
        mixed_psum = sem("mixed_psum")
        logw_ready = sem("logw_ready")
        w_ready = sem("w_ready")
        pv_psum = sem("pv_psum")
        osq_ready, ovar_psum, ovar_ready, or_ready, on_ready = (
            sem("osq_ready"), sem("ovar_psum"), sem("ovar_ready"), sem("or_ready"), sem("on_ready"))
        mix_hi_ready, mix_ready = sem("mix_hi_ready"), sem("mix_ready")
        lam_in_ready, lam_psum, lam_exp, lam_ready = sem("lam_prod"), sem("lam_psum"), sem("lam_exp"), sem("lam_ready")
        f_psum, f_ready, f_ln, logf_ready = sem("f_psum"), sem("f_ready"), sem("f_ln"), sem("logf_ready")
        cum_psum, lf_wide_ready, bias_psum, bias_ready = (
            sem("cum_psum"), sem("lf_wide_ready"), sem("bias_psum"), sem("bias_ready"))
        const_ready = sem("const_ready")
        dve_step, act_step = sem("dve_step"), sem("act_step")
        y_ready, stored = sem("y_ready"), sem("stored")

        ones = cst[:, C_ONES:C_ONES + P]
        ident = cst[:, C_IDENT:C_IDENT + P]
        later = cst[:, C_LATER:C_LATER + P]
        cum = cst[:, C_CUM:C_CUM + 2 * P]
        strict_t = cst[:, C_STRICT_T:C_STRICT_T + TRI]
        causal = cst[:, C_CAUSAL:C_CAUSAL + TRI]
        cos = cst[0:ROT, C_COS:C_COS + T]
        sin = cst[0:ROT, C_SIN:C_SIN + T]
        rot = cst[0:ROT, C_ROT:C_ROT + ROT]
        squares = wide[:].rearrange("p a b -> p (a b)")[:, 0:DT * T].rearrange("p (d t) -> p d t", d=DT)
        attn = work[:, 2:4, 0:TRI]
        s_a, s_b, s_c = (scratch[:, i, :].rearrange("p (h c) -> p h c", h=2) for i in range(3))
        gu_sb = [scratch[:, i, 0:512].rearrange("p (g t) -> p g t", g=2) for i in range(2)]
        silu_sb = [scratch[:, 2, i * T:(i + 1) * T] for i in range(2)]
        h_sb = [scratch[:, 3, i * T:(i + 1) * T] for i in range(2)]
        lf_wide = scratch[:].rearrange("p a b -> p (a b)")[:, 0:8 * T].rearrange("p (h b n) -> p h b n", h=8, b=TB)
        both = lambda a: a.unsqueeze(1).broadcast_to([a.shape[0], 2, a.shape[1]])
        flat = lambda a: a.rearrange("p a b -> p (a b)")
        halves = lambda ap: ap.rearrange("p (h t) -> p h t", h=2)

        def proj(w, c):
            return w[:, c % RING, :].rearrange("p (k n) -> p k n", k=DT)

        def down(w, c):
            return w[:, c % RING, :].rearrange("p (k n) -> p k n", k=2)

        def acc_tile(d):
            return acc[:, d // 2, (d % 2) * T:(d % 2 + 1) * T]

        def ffn_steps(run, c0):
            def first(s):
                return c0 + max(0, 3 * s - 1)
            run(0, first(0), 0)
            run(1, first(1), 0)
            yield (UNITS - 3) // 2, lambda turn: (run(2, first(2), turn), run(3, first(3), turn))
            run(UNITS - 1, first(UNITS - 1), 0)

        def slot_free(eng, c, turn=0):
            if c < RING:
                return
            c -= RING
            layer, n, c0, att, no = [p for p in phases() if p[2] <= c][-1]
            r = c - c0
            if att and r < PAIRS:
                eng.wait_ge(v_psum, layer * PAIRS + r + 1)
            elif att:
                j, kind = divmod(r - PAIRS + 1, 3) if r - PAIRS > 1 else (0, r - PAIRS)
                if r == ATT_CHUNKS - 1:
                    eng.wait_ge(acc_ready, DT * (n + 1))
                elif kind == 2:
                    eng.wait_ge(out_used, layer * (PAIRS - 1) + j)
                else:
                    eng.wait_ge(qk_psum, 2 * (layer * PAIRS + j) + kind + 1)
            else:
                u, kind = divmod(r + 1, 3) if r > 1 else (0, r)
                if r == FFN_CHUNKS - 1:
                    eng.wait_ge(acc_ready, DT * (n + 1))
                elif kind == 0:
                    eng.wait_ge(gate_used, no * UNITS + u + 1 + turn * 2)
                elif kind == 1:
                    eng.wait_ge(gu_psum, no * FFN_TILES + 2 * u + 2 + turn * 4)
                else:
                    eng.wait_ge(down_used, no * (UNITS - 1) + u + turn * 2)

        block = ctx.enter_context(nc.Block())

        @block.sync
        def _(sp):
            def load(c, chunk):
                sp.dma_start(raw[:, c % RAW, :], stream[chunk]).then_inc(raw_loaded[c % RAW], 16)

            sp.dma_start(x[:], x_in).then_inc(x_loaded, 16)
            load(0, 0)
            sp.dma_start(gain[:], gains).then_inc(const_loaded, 16)
            for c in range(1, RAW):
                load(c, c)
            sp.dma_start(cst[:], consts).then_inc(const_loaded, 16)
            sp.dma_start(lam_q[:], lam_in).then_inc(const_loaded, 16)
            sp.dma_start(subln[:], subln_in).then_inc(const_loaded, 16)
            sp.dma_start(wf[:], wf_in).then_inc(const_loaded, 16)
            sp.dma_start(bf[:], bf_in).then_inc(const_loaded, 16)
            rounds = CHUNKS // RAW - 1
            with sp.Fori(0, rounds) as turn:
                for k in range(RAW):
                    sp.wait_ge(lo_ready, turn * RAW + (k + 1))
                    load(RAW + k, turn * RAW + (RAW + k))
            for c in range((rounds + 1) * RAW, CHUNKS):
                sp.wait_ge(lo_ready, c - RAW + 1)
                load(c, c)
            for d in range(DT):
                sp.wait_ge(y_ready, d + 1)
                sp.dma_start(out[:, d, :], x[:, d, :]).then_inc(stored, 16)
            sp.wait_ge(stored, 16 * DT)

        @block.gpsimd
        def _(pool):
            nc.gpsimd.memset(half_neg[:], -0.5).then_inc(const_ready, 1)
            pool.wait_ge(const_ready, 1)
            for n in range(NORMS):
                pool.wait_ge(mean_ready, n + 1)
                nc.gpsimd.tensor_tensor(r_col[:], mean[:], half_neg[:], ALU.pow).then_inc(r_col_ready, 1)

        @block.scalar
        def _(act):
            split = [0]

            def hi(c, turn=0):
                act.wait_ge(raw_loaded[c % RAW], 16 * (c // RAW + 1) + turn * (16 * RING // RAW))
                slot_free(act, c, turn)
                nc.scalar.activation(w_hi[:, c % RING, :], raw[:, c % RAW, :], ACT.Copy).then_inc(hi_ready, 1)

            def split_to(c):
                while split[0] <= min(c, CHUNKS - 1):
                    hi(split[0])
                    split[0] += 1

            def ffn(layer, n, c0, _, f):
                def step(s, c, turn):
                    t0 = f * FFN_TILES + 2 * s
                    looped = 2 <= s < UNITS - 1
                    for k in range(2):
                        t = t0 + k
                        if looped:
                            hi(c + 3 + k, turn)
                        else:
                            split_to(c + 3 + k)
                        act.wait_ge(gu_scaled, t + 1 + turn * 4)
                        nc.scalar.activation(silu_sb[t % 2], gu_sb[t % 2][:, 0, :], ACT.Silu).then_inc(silu_ready, 1)
                        if k == 1:
                            if looped:
                                hi(c + 5, turn)
                            else:
                                split_to(c + (5 if s else 4))
                        act.wait_ge(h_ready, t + 1 + turn * 4)
                        if k == 0:
                            if s >= 2:
                                act.wait_ge(down_used, f * (UNITS - 1) + s - 1 + turn * 2)
                        nc.scalar.activation(m_hi[:, t % 4, :], h_sb[t % 2], ACT.Copy).then_inc(h_hi_ready, 1)

                for turns, body in ffn_steps(step, c0):
                    with act.Fori(0, turns) as turn:
                        body(turn)
                    split[0] = c0 + 3 * (UNITS - 2) - 1 + RING
                split_to(c0 + FFN_CHUNKS + 2)

            def attention(layer, n, c0, _, kind):
                first = layer * PAIRS
                kind = KINDS[layer]
                for c in range(PAIRS):
                    split_to(c0 + c + 3)
                    act.wait_ge(v_psum, first + c + 1)
                    if c == 0:
                        act.wait_ge(r_col_ready, n + 1)
                    for tb in range(TB):
                        ins = nc.scalar.activation(v[:, tb, c * COLS:(c + 1) * COLS], work[:, c, tb * T:(tb + 1) * T],
                                                   ACT.Identity, scale=r_col[:, tb:tb + 1])
                    ins.then_inc(v_ready, 1)
                if kind == DIFF:
                    act.wait_ge(lam_psum, 1)
                    nc.scalar.activation(lam_e[:], work[:, 3, 0:2], ACT.Exp).then_inc(lam_exp, 1)
                if kind == FOX:
                    act.wait_ge(f_ready, 1)
                    nc.scalar.activation(fg[:, 1], fg[:, 0], ACT.Abs).then_inc(act_step, 1)
                    own[0] += 1
                    act.wait_ge(act_step, own[0])
                    nc.scalar.activation(fg[:, 1], fg[:, 1], ACT.Exp, scale=-1.0).then_inc(act_step, 1)
                    own[0] += 1
                    act.wait_ge(act_step, own[0])
                    nc.scalar.activation(fg[:, 2], fg[:, 1], ACT.Ln, bias=1.0).then_inc(f_ln, 1)
                for j in range(PAIRS + 1):
                    a = first + j
                    q_chunk = c0 + PAIRS + (3 * j - 1 if j else 0)
                    if j < PAIRS:
                        split_to(q_chunk + 3)
                    if j:
                        b = a - 1
                        if kind == STICK:
                            act.wait_ge(logw_ready, KINDS[:layer].count(STICK) * PAIRS + j)
                            nc.scalar.activation(w_t[:], s_b, ACT.Exp).then_inc(w_ready, 1)
                        elif kind == FOX:
                            act.wait_ge(mixed_psum, b + 1)
                            nc.scalar.activation(w_t[:], attn, ACT.Copy).then_inc(w_ready, 1)
                        else:
                            act.wait_ge(mixed_psum, b + 1)
                            nc.scalar.activation(w_t[:, 0, :], work[:, 2, 0:TRI], ACT.Copy).then_inc(w_ready, 1)
                        if j < PAIRS:
                            split_to(q_chunk + 4)
                        act.wait_ge(pv_psum, b + 1)
                        slot = 2 * (b % 2)
                        pair = m_hi[:, slot:slot + 2, :]
                        if kind == DIFF:
                            nc.scalar.activation(scratch[:, 2, 0:512], work[:, 0, :],
                                                 ACT.Square).then_inc(osq_ready, 1)
                            act.wait_ge(ovar_ready, j)
                            nc.scalar.activation(scratch[:, 2, 0:T], scratch[:, 2, 0:T], ACT.Ln).then_inc(act_step, 1)
                            own[0] += 1
                            act.wait_ge(act_step, own[0])
                            nc.scalar.activation(scratch[:, 2, 0:T], scratch[:, 2, 0:T], ACT.Exp,
                                                 scale=-0.5).then_inc(or_ready, 1)
                            act.wait_ge(on_ready, j)
                            for h in range(2):
                                ins = nc.scalar.activation(m_hi[:, slot + h, :], scratch[:, 3, h * T:(h + 1) * T],
                                                           ACT.Identity, scale=subln_s[:, h:h + 1])
                            ins.then_inc(mix_hi_ready, 1)
                        else:
                            nc.scalar.activation(pair, halves(work[:, 0, :]), ACT.Copy).then_inc(mix_hi_ready, 1)
                    if j < PAIRS:
                        split_to(q_chunk + 5)
                        act.wait_ge(scores_ready, a + 1)
                        if kind == STICK:
                            nc.scalar.activation(s_b, s_a, ACT.Abs).then_inc(act_step, 1)
                            own[0] += 1
                            act.wait_ge(act_step, own[0])
                            nc.scalar.activation(s_b, s_b, ACT.Exp, scale=-1.0).then_inc(act_step, 1)
                            own[0] += 1
                            act.wait_ge(act_step, own[0])
                            nc.scalar.activation(s_c, s_b, ACT.Ln, bias=1.0).then_inc(exp_ready, 1)
                        else:
                            for h in range(2):
                                for tb in range(TB):
                                    cols = slice(0, P) if tb == 0 else slice(P, TRI)
                                    ins = nc.scalar.activation(s_b[:, h, cols], s_a[:, h, cols], ACT.Exp,
                                                               bias=neg_max[:, h, tb:tb + 1],
                                                               accum_out=row_sum[:, h, tb:tb + 1])
                            ins.then_inc(exp_ready, 1)
                split_to(c0 + ATT_CHUNKS + 3)

            def gains_and_squares(n, before_squares=-1):
                for d in range(DT):
                    if n:
                        act.wait_ge(x_updated, DT * (n - 1) + d + 1)
                    if n < NORMS - 1:
                        nc.scalar.activation(xg_hi[:, d, :], x[:, d, :], ACT.Identity,
                                             scale=gain[:, n, d:d + 1]).then_inc(xg_hi_ready, 1)
                split_to(before_squares)
                for d in range(0, DT, 2):
                    ins = nc.scalar.activation(squares[:, d:d + 2, :], x[:, d:d + 2, :], ACT.Square)
                ins.then_inc(squares_ready, 1)

            own = [0]
            act.wait_ge(x_loaded, 16)
            act.wait_ge(const_loaded, 16 * 6)
            gains_and_squares(0, 1)
            for phase in phases():
                (attention if phase[3] else ffn)(*phase)
                gains_and_squares(phase[1] + 1)

        @block.vector
        def _(dve):
            split = [0]
            own = [0]

            def done(ins):
                own[0] += 1
                ins.then_inc(dve_step, 1)
                dve.wait_ge(dve_step, own[0])

            def lo(c, turn=0):
                dve.wait_ge(hi_ready, c + 1 + turn * RING)
                nc.vector.tensor_tensor(w_lo[:, c % RING, :], raw[:, c % RAW, :], w_hi[:, c % RING, :].bitcast(F32),
                                        ALU.subtract).then_inc(lo_ready, 1)

            def split_to(c):
                while split[0] <= min(c, CHUNKS - 1):
                    lo(split[0])
                    split[0] += 1

            def norm_sums(n):
                dve.wait_ge(squares_ready, n + 1)
                done(nc.vector.tensor_tensor(squares[:, 0:4, :], squares[:, 0:4, :], squares[:, 4:8, :], ALU.add))
                done(nc.vector.tensor_tensor(squares[:, 0:2, :], squares[:, 0:2, :], squares[:, 2:4, :], ALU.add))
                nc.vector.tensor_tensor(squares[:, 0, :], squares[:, 0, :], squares[:, 1, :],
                                        ALU.add).then_inc(square_sum_ready, 1)

            def norm_mean(n):
                dve.wait_ge(var_ready, n + 1)
                nc.vector.tensor_scalar(mean[:], acc[:, 0, 0:TB], 1.0 / D, EPS, ALU.mult, ALU.add).then_inc(mean_ready, 1)

            def norm_diag(n):
                dve.wait_ge(r_col_ready, n + 1)
                for tb in range(TB):
                    ins = nc.vector.tensor_scalar(r_diag[:, tb * P:(tb + 1) * P], ident, r_col[:, tb:tb + 1], None,
                                                  ALU.mult)
                ins.then_inc(r_diag_ready, 1)

            def norm_row(n):
                dve.wait_ge(r_row_psum, n + 1)
                nc.vector.tensor_copy(r_row[:], acc[:, 1, 0:T]).then_inc(r_row_ready, 1)

            def ffn(layer, n, c0, _, f):
                norm_sums(n)
                split_to(c0 + 2)
                norm_mean(n)
                split_to(c0 + 3)
                norm_diag(n)
                norm_row(n)
                dve.wait_ge(r_row_ready, n + 1)

                def step(s, c, turn):
                    t0 = f * FFN_TILES + 2 * s
                    looped = 2 <= s < UNITS - 1

                    def split_next(k):
                        if looped:
                            lo(c + 3 + k, turn)
                        else:
                            split_to(c + (3 + k if s else 2 + k))

                    for k in range(2):
                        t = t0 + k
                        dve.wait_ge(gu_psum, t + 1 + turn * 4)
                        nc.vector.tensor_tensor(gu_sb[t % 2], halves(work[:, t % 4, :]), both(r_row[:]),
                                                ALU.mult).then_inc(gu_scaled, 1)
                        split_next(2 * k)
                        dve.wait_ge(silu_ready, t + 1 + turn * 4)
                        nc.vector.tensor_tensor(h_sb[t % 2], silu_sb[t % 2], gu_sb[t % 2][:, 1, :],
                                                ALU.mult).then_inc(h_ready, 1)
                        if k == 0:
                            split_next(1)
                        dve.wait_ge(h_hi_ready, t + 1 + turn * 4)
                        nc.vector.tensor_tensor(m_lo[:, t % 4, :], h_sb[t % 2], m_hi[:, t % 4, :].bitcast(F32),
                                                ALU.subtract).then_inc(h_split, 1)

                for turns, body in ffn_steps(step, c0):
                    with dve.Fori(0, turns) as turn:
                        body(turn)
                    split[0] = c0 + 3 * (UNITS - 2) - 1 + RING
                split_to(c0 + FFN_CHUNKS + 2)

            def attention(layer, n, c0, _, kind):
                kind = KINDS[layer]
                first = layer * PAIRS
                norm_sums(n)
                split_to(c0 + 3)
                norm_mean(n)
                norm_diag(n)
                norm_row(n)
                split_to(c0 + 4)
                if kind == DIFF:
                    lp = lam_q[:].rearrange("p (a b) -> p a b", b=2)
                    nc.vector.tensor_tensor(lam_p[:], lp[:, :, 0], lp[:, :, 1], ALU.mult).then_inc(lam_in_ready, 1)
                    nc.vector.tensor_scalar(subln_s[:], subln[:], 1.0 - LAM_INIT, None, ALU.mult)
                    dve.wait_ge(lam_exp, 1)
                    done(nc.vector.tensor_tensor(lam[:, 0:1], lam_e[:, 0:1], lam_e[:, 1:2], ALU.subtract))
                    done(nc.vector.tensor_scalar(lam[:, 1:2], lam[:, 0:1], LAM_INIT, None, ALU.add))
                if kind == FOX:
                    dve.wait_ge(f_psum, 1)
                    for tb in range(TB):
                        ins = nc.vector.scalar_tensor_tensor(
                            out=fg[:, 0, tb, :], in0=work[:, 3, tb * 8:(tb + 1) * 8], scalar=r_col[:, tb:tb + 1],
                            in1=bf[:], op0=ALU.mult, op1=ALU.add)
                    ins.then_inc(f_ready, 1)
                    dve.wait_ge(f_ln, 1)
                    nc.vector.scalar_tensor_tensor(out=flat(fg[:, 3]), in0=flat(fg[:, 0]), scalar=0.0,
                                                   in1=flat(fg[:, 2]), op0=ALU.min,
                                                   op1=ALU.subtract).then_inc(logf_ready, 1)
                dve.wait_ge(r_row_ready, n + 1)

                def forget_cums():
                    dve.wait_ge(cum_psum, 1)
                    nc.vector.tensor_copy(flat(cum_col[:]), work[:, 3, 0:2 * 8])
                    for head in range(2 * PAIRS):
                        for tb in range(TB):
                            ins = nc.vector.tensor_scalar(lf_wide[:, head, tb, :], ones, fg[:, 3, tb, head:head + 1],
                                                          None, ALU.mult)
                    ins.then_inc(lf_wide_ready, 1)

                def forget_bias():
                    for pair in range(PAIRS):
                        dve.wait_ge(bias_psum, pair + 1)
                        for h in range(2):
                            bank = work[:, 2 + pair % 2, h * T:(h + 1) * T]
                            head = 2 * pair + h
                            nc.vector.tensor_tensor(wide[:, head, 0:P], causal[:, 0:P], bank[:, 0:P], ALU.subtract)
                            ins = nc.vector.tensor_tensor(wide[:, head, P:TRI], causal[:, P:TRI], bank, ALU.subtract)
                        ins.then_inc(bias_ready, 1)
                    dve.wait_ge(bias_ready, PAIRS)

                def scale_qk(dst, bank, count, scale):
                    dve.wait_ge(qk_psum, count)
                    src = halves(work[:, bank, :])
                    rotate = kind == DIFF
                    ins = nc.vector.scalar_tensor_tensor(out=dst[:], in0=src, scalar=scale, in1=both(r_row[:]),
                                                         op0=ALU.mult, op1=ALU.mult)
                    ins.then_inc(rope_in if rotate else qk_ready, 1)
                    if rotate:
                        k = count - 2 * first
                        dve.wait_ge(rope_in, k)
                        turned = scratch[0:ROT, 3, 0:512]
                        dve.wait_ge(rope_psum, k)
                        nc.vector.tensor_tensor(halves(turned), halves(work[0:ROT, bank, :]), both(sin), ALU.mult)
                        done(nc.vector.tensor_tensor(dst[0:ROT], dst[0:ROT], both(cos), ALU.mult))
                        nc.vector.tensor_tensor(dst[0:ROT], dst[0:ROT], halves(turned), ALU.add).then_inc(qk_ready, 1)

                for j in range(PAIRS + 1):
                    a = first + j
                    q_chunk = c0 + PAIRS + (3 * j - 1 if j else 0)
                    if j < PAIRS:
                        split_to(q_chunk + 3)
                        scale_qk(q_t, 0, 2 * a + 1, SCALE)
                        if kind == FOX and j == 0:
                            forget_cums()
                    if j:
                        b = a - 1
                        if kind == STICK:
                            dve.wait_ge(mixed_psum, b + 1)
                            nc.vector.tensor_tensor(s_b, s_a, attn, ALU.subtract).then_inc(logw_ready, 1)
                        if j < PAIRS:
                            split_to(q_chunk + 4)
                    if j < PAIRS:
                        scale_qk(k_t, 1, 2 * a + 2, 1.0)
                        if kind == FOX and j == 0:
                            forget_bias()
                    if j:
                        slot = 2 * (b % 2)
                        if kind == DIFF:
                            dve.wait_ge(ovar_psum, j)
                            nc.vector.tensor_scalar(scratch[:, 2, 0:T], work[:, 1, 0:T], 1.0 / COLS, EPS, ALU.mult,
                                                    ALU.add).then_inc(ovar_ready, 1)
                            dve.wait_ge(or_ready, j)
                            nc.vector.tensor_tensor(halves(scratch[:, 3, 0:512]), halves(work[:, 0, :]),
                                                    both(scratch[:, 2, 0:T]), ALU.mult).then_inc(on_ready, 1)
                            dve.wait_ge(mix_hi_ready, b + 1)
                            for h in range(2):
                                ins = nc.vector.scalar_tensor_tensor(
                                    out=m_lo[:, slot + h, :], in0=scratch[:, 3, h * T:(h + 1) * T],
                                    scalar=subln_s[:, h:h + 1], in1=m_hi[:, slot + h, :].bitcast(F32),
                                    op0=ALU.mult, op1=ALU.subtract)
                            ins.then_inc(mix_ready, 1)
                        else:
                            dve.wait_ge(mix_hi_ready, b + 1)
                            nc.vector.tensor_tensor(m_lo[:, slot:slot + 2, :], halves(work[:, 0, :]),
                                                    m_hi[:, slot:slot + 2, :].bitcast(F32),
                                                    ALU.subtract).then_inc(mix_ready, 1)
                    if j < PAIRS:
                        dve.wait_ge(scores_psum, a + 1)
                        if kind == STICK:
                            nc.vector.tensor_tensor(s_a, attn, both(strict_t), ALU.add).then_inc(scores_ready, 1)
                            split_to(q_chunk + 5)
                            dve.wait_ge(exp_ready, a + 1)
                            nc.vector.scalar_tensor_tensor(out=s_c, in0=s_a, scalar=0.0, in1=s_c, op0=ALU.max,
                                                           op1=ALU.add).then_inc(mix_in, 1)
                            continue
                        if kind == DIFF:
                            ins = nc.vector.tensor_tensor(s_a, attn, both(causal), ALU.add)
                        else:
                            for h in range(2):
                                head = 2 * j + h
                                for tb in range(TB):
                                    cols = slice(0, P) if tb == 0 else slice(P, TRI)
                                    ins = nc.vector.scalar_tensor_tensor(
                                        out=s_a[:, h, cols], in0=work[:, 2 + h, cols], scalar=cum_col[:, tb, head:head + 1],
                                        in1=wide[:, head, cols], op0=ALU.add, op1=ALU.add)
                        done(ins)
                        nc.vector.tensor_reduce(row_max[:, :, 0], s_a[:, :, 0:P], AX_X, ALU.max)
                        done(nc.vector.tensor_reduce(row_max[:, :, 1], s_a[:, :, P:TRI], AX_X, ALU.max))
                        nc.vector.tensor_scalar(neg_max[:], row_max[:], -1.0, None, ALU.mult).then_inc(scores_ready, 1)
                        split_to(q_chunk + 5)
                        dve.wait_ge(exp_ready, a + 1)
                        done(nc.vector.reciprocal(row_inv[:], row_sum[:]))
                        if kind == FOX:
                            for h in range(2):
                                for tb in range(TB):
                                    cols = slice(0, P) if tb == 0 else slice(P, TRI)
                                    ins = nc.vector.tensor_scalar(s_a[:, h, cols], s_b[:, h, cols],
                                                                  row_inv[:, h, tb:tb + 1], None, ALU.mult)
                            ins.then_inc(mix_in, 1)
                            continue
                        for tb in range(TB):
                            cols = slice(0, P) if tb == 0 else slice(P, TRI)
                            ins = nc.vector.tensor_scalar(s_a[:, 1, cols], s_b[:, 1, cols], row_inv[:, 1, tb:tb + 1],
                                                          lam[:, 1:2], ALU.mult, ALU.mult)
                        done(ins)
                        for tb in range(TB):
                            cols = slice(0, P) if tb == 0 else slice(P, TRI)
                            ins = nc.vector.scalar_tensor_tensor(
                                out=s_a[:, 0, cols], in0=s_b[:, 0, cols], scalar=row_inv[:, 0, tb:tb + 1],
                                in1=s_a[:, 1, cols], op0=ALU.mult, op1=ALU.subtract)
                        ins.then_inc(mix_in, 1)
                split_to(c0 + ATT_CHUNKS + 3)

            def update(n, scale):
                def lo_half(d):
                    dve.wait_ge(xg_hi_ready, DT * n + d + 1)
                    nc.vector.scalar_tensor_tensor(out=xg_lo[:, d, :], in0=x[:, d, :], scalar=gain[:, n, d:d + 1],
                                                   in1=xg_hi[:, d, :].bitcast(F32), op0=ALU.mult,
                                                   op1=ALU.subtract).then_inc(xg_ready, 1)

                for d in range(DT + 1):
                    if d < DT and n:
                        if d % 2 == 0:
                            dve.wait_ge(acc_ready, DT * (n - 1) + d + 2)
                        nc.vector.scalar_tensor_tensor(out=x[:, d, :], in0=acc_tile(d), scalar=scale, in1=x[:, d, :],
                                                       op0=ALU.mult, op1=ALU.add).then_inc(x_updated, 1)
                    if d and n < NORMS - 1:
                        lo_half(d - 1)

            dve.wait_ge(x_loaded, 16)
            dve.wait_ge(const_loaded, 16 * 6)
            update(0, 1.0)
            split_to(1)
            for phase in phases():
                (attention if phase[3] else ffn)(*phase)
                update(phase[1] + 1, 1.0 if phase[3] else 0.5)

            n = NORMS - 1
            norm_sums(n)
            norm_mean(n)
            norm_diag(n)
            norm_row(n)
            dve.wait_ge(r_row_ready, n + 1)
            for d in range(DT):
                nc.vector.scalar_tensor_tensor(out=x[:, d, :], in0=x[:, d, :], scalar=gain[:, n, d:d + 1],
                                               in1=r_row[:], op0=ALU.mult, op1=ALU.mult).then_inc(y_ready, 1)

        @block.tensor
        def _(pe):
            def product(dst, a_hi, a_lo, b_hi, b_lo, start, stop, skip=False):
                nc.tensor.matmul(dst, a_hi, b_hi, start=start, stop=False, skip_group_check=skip)
                nc.tensor.matmul(dst, a_hi, b_lo, start=False, stop=False, skip_group_check=skip)
                return nc.tensor.matmul(dst, a_lo, b_hi, start=False, stop=stop, skip_group_check=skip)

            def project(dst, c, col, xg_first=None):
                for k in range(DT):
                    if xg_first is not None:
                        pe.wait_ge(xg_ready, DT * xg_first + k + 1)
                    ins = product(dst, proj(w_hi, c)[:, k, col:col + P], proj(w_lo, c)[:, k, col:col + P],
                                  xg_hi[:, k, :], xg_lo[:, k, :], start=k == 0, stop=k == DT - 1)
                return ins

            def contract_pair(c, slot, first, last):
                for t in range(2):
                    for d in range(DT):
                        ins = product(acc_tile(d), down(w_hi, c)[:, t, d * P:(d + 1) * P],
                                      down(w_lo, c)[:, t, d * P:(d + 1) * P], m_hi[:, slot + t, :], m_lo[:, slot + t, :],
                                      start=first and t == 0 and d % 2 == 0, stop=last and t == 1, skip=True)
                        if last and t == 1:
                            ins.then_inc(acc_ready, 1)
                return ins

            def norm_var(n):
                pe.wait_ge(square_sum_ready, n + 1)
                for tb in range(TB):
                    ins = nc.tensor.matmul(acc[:, 0, tb:tb + 1], squares[:, 0, tb * P:(tb + 1) * P], ones[:, 0:1],
                                           start=True, stop=True)
                ins.then_inc(var_ready, 1)

            def norm_row(n):
                pe.wait_ge(r_diag_ready, n + 1)
                nc.tensor.matmul(acc[:, 1, 0:T], ones, r_diag[:], start=True, stop=True).then_inc(r_row_psum, 1)

            def ffn(layer, n, c0, _, f):
                def step(s, c, turn):
                    pe.wait_ge(lo_ready, c + 2 + turn * RING)
                    for k in range(2):
                        t = f * FFN_TILES + 2 * s + k
                        if s >= 2:
                            pe.wait_ge(gu_scaled, t - 3 + turn * 4)
                        ins = project(work[:, t % 4, 0:T], c, k * P, n if s == 0 and k == 0 else None)
                        if k == 1:
                            ins.then_inc(gate_used, 1)
                        project(work[:, t % 4, T:2 * T], c + 1, k * P).then_inc(gu_psum, 1)
                        if s == 0:
                            (norm_row if k else norm_var)(n)
                    if s:
                        unit_down(s - 1, c + 2, turn).then_inc(down_used, 1)

                def unit_down(u, c, turn, last=False):
                    pe.wait_ge(lo_ready, c + 1 + turn * RING)
                    pe.wait_ge(h_split, f * FFN_TILES + 2 * u + 2 + turn * 4)
                    return contract_pair(c, (f * FFN_TILES + 2 * u) % 4, u == 0, last)

                for turns, body in ffn_steps(step, c0):
                    with pe.Fori(0, turns) as turn:
                        body(turn)
                unit_down(UNITS - 1, c0 + FFN_CHUNKS - 1, 0, True)

            def attention(layer, n, c0, _, kind):
                kind = KINDS[layer]
                first = layer * PAIRS

                for c in range(PAIRS):
                    pe.wait_ge(lo_ready, c0 + c + 1)
                    for tb in range(TB):
                        for k in range(DT):
                            if c == tb == 0:
                                pe.wait_ge(xg_ready, DT * n + k + 1)
                            ins = product(work[:, c, tb * T:(tb + 1) * T], xg_hi[:, k, tb * P:(tb + 1) * P],
                                          xg_lo[:, k, tb * P:(tb + 1) * P], proj(w_hi, c0 + c)[:, k, :],
                                          proj(w_lo, c0 + c)[:, k, :], start=k == 0, stop=k == DT - 1)
                    ins.then_inc(v_psum, 1)
                    if c == 0:
                        norm_var(n)
                    if c == 1:
                        norm_row(n)
                pe.wait_ge(v_ready, first + PAIRS)
                if kind == DIFF:
                    pe.wait_ge(lam_in_ready, 1)
                    nc.tensor.matmul(work[:, 3, 0:2], ones, lam_p[:], start=True, stop=True).then_inc(lam_psum, 1)
                if kind == FOX:
                    for tb in range(TB):
                        for k in range(DT):
                            for part in (xg_hi, xg_lo):
                                ins = nc.tensor.matmul(
                                    work[:, 3, tb * 8:(tb + 1) * 8], part[:, k, tb * P:(tb + 1) * P].bitcast(F32),
                                    wf[:, k, :], start=k == 0 and part is xg_hi, stop=k == DT - 1 and part is xg_lo)
                    ins.then_inc(f_psum, 1)

                def queries_or_keys(c, bank):
                    pe.wait_ge(lo_ready, c + 1)
                    project(work[:, bank, 0:T], c, 0)
                    project(work[:, bank, T:2 * T], c, P).then_inc(qk_psum, 1)

                def rotate(t, bank, j, k):
                    pe.wait_ge(rope_in, 2 * j + k)
                    nc.tensor.matmul(work[0:ROT, bank, :], rot, flat(t[0:ROT]), start=True,
                                     stop=True).then_inc(rope_psum, 1)

                def forget_cums():
                    pe.wait_ge(logf_ready, 1)
                    nc.tensor.matmul(work[:, 3, 0:8], cum[:, 0:P], fg[:, 3, 0, :], start=True, stop=True)
                    nc.tensor.matmul(work[:, 3, 8:16], ones, fg[:, 3, 0, :], start=True, stop=False)
                    nc.tensor.matmul(work[:, 3, 8:16], cum[:, 0:P], fg[:, 3, 1, :], start=False,
                                     stop=True).then_inc(cum_psum, 1)

                def forget_bias():
                    pe.wait_ge(lf_wide_ready, 1)
                    for pair in range(PAIRS):
                        if pair >= 2:
                            pe.wait_ge(bias_ready, pair - 1)
                        for h in range(2):
                            bank, head = work[:, 2 + pair % 2, h * T:(h + 1) * T], 2 * pair + h
                            nc.tensor.matmul(bank, lf_wide[:, head, 0, :], cum, start=True, stop=True)
                            ins = nc.tensor.matmul(bank[:, P:T], lf_wide[:, head, 1, :], cum[:, 0:P], start=False,
                                                   stop=True, skip_group_check=True)
                        ins.then_inc(bias_psum, 1)
                    pe.wait_ge(bias_ready, PAIRS)

                def scores(a):
                    pe.wait_ge(qk_ready, 2 * a + 2)
                    for h in range(2):
                        q, k, bank = q_t[:, h, :], k_t[:, h, :], work[:, 2 + h, :]
                        if kind == STICK:
                            nc.tensor.matmul(bank[:, 0:T], k[:, 0:P], q, start=True, stop=True)
                            ins = nc.tensor.matmul(bank[:, T:TRI], k[:, P:T], q[:, P:T], start=True, stop=True)
                        else:
                            nc.tensor.matmul(bank[:, 0:P], q[:, 0:P], k[:, 0:P], start=True, stop=True)
                            ins = nc.tensor.matmul(bank[:, P:TRI], q[:, P:T], k, start=True, stop=True)
                    ins.then_inc(scores_psum, 1)

                def mixed(b):
                    pe.wait_ge(mix_in, b + 1)
                    for h in range(1 if kind == DIFF else 2):
                        bank = work[:, 2 + h, :]
                        if kind == STICK:
                            nc.tensor.matmul(bank[:, 0:TRI], later, s_c[:, h, :], start=True, stop=True)
                            ins = nc.tensor.matmul(bank[:, P:T], ones, s_c[:, h, T:TRI], start=False, stop=True,
                                                   skip_group_check=True)
                        else:
                            for at in range(0, TRI, P):
                                ins = nc.tensor.transpose(bank[:, at:at + P], s_a[:, h, at:at + P], ident)
                    ins.then_inc(mixed_psum, 1)

                def weighted_values(b):
                    pe.wait_ge(w_ready, b + 1)
                    for h in range(2):
                        bank, cols = work[:, 0, h * T:(h + 1) * T], slice((2 * (b - first) + h) * HD, (2 * (b - first) + h + 1) * HD)
                        w = w_t[:, 0 if kind == DIFF else h, :]
                        nc.tensor.matmul(bank, v[:, 0, cols], w[:, 0:T], start=True, stop=True)
                        ins = nc.tensor.matmul(bank[:, P:T], v[:, 1, cols], w[:, T:TRI], start=False, stop=True,
                                               skip_group_check=True)
                    ins.then_inc(pv_psum, 1)

                def output_squares(j):
                    pe.wait_ge(osq_ready, j)
                    nc.tensor.matmul(work[:, 1, 0:T], ones, scratch[:, 2, 0:T], start=True, stop=False)
                    nc.tensor.matmul(work[:, 1, 0:T], ones, scratch[:, 2, T:2 * T], start=False,
                                     stop=True).then_inc(ovar_psum, 1)

                for j in range(PAIRS + 1):
                    a, b = first + j, first + j - 1
                    c = c0 + PAIRS + (3 * j - 1 if j else 0)
                    if j < PAIRS:
                        queries_or_keys(c, 0)
                        if kind == FOX and j == 0:
                            forget_cums()
                    if j:
                        mixed(b)
                    if j < PAIRS:
                        if kind == DIFF:
                            rotate(q_t, 0, j, 1)
                        queries_or_keys(c + 1, 1)
                        if kind == FOX and j == 0:
                            forget_bias()
                    if j:
                        if j < PAIRS:
                            pe.wait_ge(qk_ready, 2 * a + 1)
                        weighted_values(b)
                    if kind == DIFF and j < PAIRS:
                        rotate(k_t, 1, j, 2)
                        pe.wait_ge(qk_ready, 2 * a + 2)
                    if j and kind == DIFF:
                        output_squares(j)
                    if j < PAIRS:
                        scores(a)
                    if j:
                        c = c + 2 if j < PAIRS else c0 + ATT_CHUNKS - 1
                        pe.wait_ge(lo_ready, c + 1)
                        pe.wait_ge(mix_ready, b + 1)
                        ins = contract_pair(c, 2 * (b % 2), j == 1, j == PAIRS)
                        if j < PAIRS:
                            ins.then_inc(out_used, 1)

            pe.wait_ge(const_loaded, 16 * 6)
            for phase in phases():
                (attention if phase[3] else ffn)(*phase)
            norm_var(NORMS - 1)
            norm_row(NORMS - 1)


def kernel(x, norm_g, final_g, ffn_w_gate, ffn_w_up, ffn_w_down, w_qkv, w_o,
           diff_lambda, diff_subln_g, fox_w_f, fox_b_f):
    import concourse.bacc as bacc
    from concourse.bass_utils import run_bass_kernel_spmd

    a = [np.asarray(w) for w in (ffn_w_gate, ffn_w_up, ffn_w_down, w_qkv, w_o)]
    gate, up, down_w, qkv, w_out = a
    stream = np.empty((CHUNKS, P, CHUNK), np.float32)
    columns = lambda w, u: w[:, u * COLS:(u + 1) * COLS].reshape(DT, P, COLS).transpose(1, 0, 2).reshape(P, CHUNK)
    rows = lambda w, u: w[u * 2 * P:(u + 1) * 2 * P].reshape(2, P, D).transpose(1, 0, 2).reshape(P, CHUNK)
    chunks = []
    for layer in range(DEPTH):
        for part in range(3):
            if part == 1:
                w = qkv[layer]
                q, k, v = w[:, :D], w[:, D:2 * D], w[:, 2 * D:]
                chunks += [columns(v, j) for j in range(PAIRS)]
                for j in range(PAIRS):
                    chunks += [columns(q, j), columns(k, j)]
                    if j:
                        chunks.append(rows(w_out[layer], j - 1))
                chunks.append(rows(w_out[layer], PAIRS - 1))
            else:
                w = layer, part // 2
                for u in range(UNITS):
                    chunks += [columns(gate[w], u), columns(up[w], u)]
                    if u:
                        chunks.append(rows(down_w[w], u - 1))
                chunks.append(rows(down_w[w], UNITS - 1))
    for c, chunk in enumerate(chunks):
        stream[c] = chunk
    tiles = lambda t: np.ascontiguousarray(np.asarray(t).reshape(DT, P, -1).transpose(1, 0, 2))
    gains = np.concatenate([np.asarray(norm_g).reshape(3 * DEPTH, D), np.asarray(final_g).reshape(1, D)])
    arrays = {
        "stream": stream,
        "x": tiles(np.asarray(x)[0].T),
        "gains": np.ascontiguousarray(gains.reshape(NORMS, DT, P).transpose(2, 0, 1)),
        "consts": constants(),
        "lam": np.ascontiguousarray(np.asarray(diff_lambda)[0].T),
        "subln": np.ascontiguousarray(np.asarray(diff_subln_g)[0].reshape(2, P).T),
        "wf": tiles(np.asarray(fox_w_f)[0]),
        "bf": np.ascontiguousarray(np.broadcast_to(np.asarray(fox_b_f)[0], (P, 8))),
    }
    nc = bacc.Bacc("TRN2", target_bir_lowering=False, num_devices=1)
    args = [nc.dram_tensor(f"{name}_dram", arr.shape, F32, kind="ExternalInput").ap() for name, arr in arrays.items()]
    out = nc.dram_tensor("out_dram", (P, DT, T), F32, kind="ExternalOutput").ap()
    trunk(nc, *args, out)
    y = run_bass_kernel_spmd(nc, [{f"{name}_dram": arr for name, arr in arrays.items()}], core_ids=[0]).results[0]["out_dram"]
    return np.ascontiguousarray(y.transpose(2, 1, 0).reshape(1, T, D))
```

```python
import math
from contextlib import ExitStack

import numpy as np

import concourse.bass as bass
from concourse import mybir

F32 = mybir.dt.float32
F32R = mybir.dt.float32r
ALU = mybir.AluOpType
ACT = mybir.ActivationFunctionType
AX_X = mybir.AxisListType.X

P = 128
D, T, FF, DEPTH = 1024, 256, 2816, 4
HD = 128
DT = D // P
TB = T // P
COLS = 256
CHUNK = DT * COLS
UNITS = FF // COLS
PAIRS = D // COLS
FFN_CHUNKS = 3 * UNITS
ATT_CHUNKS = 4 * PAIRS
CHUNKS = DEPTH * (2 * FFN_CHUNKS + ATT_CHUNKS)
FFN_TILES = 2 * UNITS
NORMS = 3 * DEPTH + 1
NORM_AT = 5
RAW = 3
RING = 6
SCALE = HD ** -0.5
EPS = 1e-6
NEG = -1e30
TRI = T + P
ROWS = slice(0, P), slice(P, TRI)
STICK, DIFF, FOX = range(3)
KINDS = [i % 3 for i in range(DEPTH)]
ROT = 32
LAM_INIT = 0.8 - 0.6 * math.exp(-0.3 * KINDS.index(DIFF))

C_ONES, C_IDENT, C_LATER, C_CUM = 0, 128, 256, 384
C_STRICT_T, C_CAUSAL, C_COS, C_SIN, C_ROT = 640, 1024, 1408, 1664, 1920
C_END = 1952


ATT_ORDER = ([("v", j) for j in range(PAIRS)] + [("q", 0), ("k", 0), ("q", 1), ("k", 1)]
             + [x for j in range(2, PAIRS) for x in (("q", j), ("k", j), ("o", j - 2))]
             + [("o", PAIRS - 2), ("o", PAIRS - 1)])
FFN_ORDER = ([("gate", 0), ("up", 0)] + [x for u in range(1, UNITS) for x in (("gate", u), ("up", u), ("down", u - 1))]
             + [("down", UNITS - 1)])


def constants():
    c = np.zeros((P, C_END), np.float32)
    a = np.arange(P)
    c[:, C_ONES:C_ONES + P] = 1.0
    c[:, C_IDENT:C_IDENT + P] = np.eye(P)
    c[:, C_LATER:C_LATER + P] = a[:, None] >= a[None, :]
    c[:, C_CUM:C_CUM + P] = a[:, None] <= a[None, :]
    c[:, C_CUM + P:C_CUM + 2 * P] = 1.0
    strict = np.where(a[:, None] < a[None, :], 0.0, NEG)
    causal = np.where(a[None, :] <= a[:, None], 0.0, NEG)
    for at, mask in ((C_STRICT_T, strict), (C_CAUSAL, causal)):
        c[:, at:at + P] = mask
        c[:, at + 2 * P:at + 3 * P] = mask
    half = ROT // 2
    inv = np.float32(500000.0) ** (-np.arange(half, dtype=np.float32) * np.float32(2.0) / np.float32(ROT))
    ang = (np.arange(T, dtype=np.float32)[:, None] * inv[None, :].astype(np.float32)).astype(np.float64).T
    for at, f in ((C_COS, np.cos), (C_SIN, np.sin)):
        c[0:half, at:at + T] = f(ang)
        c[half:ROT, at:at + T] = f(ang)
    for m in range(half):
        c[m + half, C_ROT + m] = -1.0
        c[m, C_ROT + m + half] = 1.0
    return c


def phases():
    out, chunk, ffn = [], 0, 0
    for layer in range(DEPTH):
        for part in range(3):
            att = part == 1
            out.append((layer, 3 * layer + part, chunk, att, layer if att else ffn))
            chunk += ATT_CHUNKS if att else FFN_CHUNKS
            ffn += not att
    return out


def trunk(nc, stream, x_in, gains, consts, lam_in, subln_in, wf_in, bf_in, out):
    with ExitStack() as ctx:
        def sb(name, shape, dt=F32):
            return ctx.enter_context(nc.sbuf_tensor(name, shape, dt))

        def sem(name):
            return ctx.enter_context(nc.semaphore(name))

        raw = sb("raw", [P, RAW, CHUNK])
        w_hi = sb("w_hi", [P, RING, CHUNK], F32R)
        w_lo = sb("w_lo", [P, RING, CHUNK], F32R)
        x = sb("x", [P, DT, T])
        xg_hi = sb("xg_hi", [P, DT, T], F32R)
        xg_lo = sb("xg_lo", [P, DT, T], F32R)
        m_hi = sb("m_hi", [P, 4, T], F32R)
        m_lo = sb("m_lo", [P, 4, T], F32R)
        scratch = sb("scratch", [P, 4, 2 * TRI])
        wide = sb("wide", [P, DT, TRI])
        v = sb("v", [P, TB, D])
        q_t = sb("q_t", [P, 2, T])
        k_t = sb("k_t", [P, 2, T])
        w_t = sb("w_t", [P, 2, TRI])
        cst = sb("cst", [P, C_END])
        gain = sb("gain", [P, NORMS, DT])
        r_row = sb("r_row", [P, T])
        r_diag = sb("r_diag", [P, T])
        mean = sb("mean", [P, TB])
        r_col = sb("r_col", [P, TB])
        half_neg = sb("half_neg", [P, TB])
        row_max = sb("row_max", [P, 2, TB])
        neg_max = sb("neg_max", [P, 2, TB])
        row_sum = sb("row_sum", [P, 2, TB])
        row_inv = sb("row_inv", [P, 2, TB])
        lam_q = sb("lam_q", [P, 4])
        lam_p = sb("lam_p", [P, 2])
        lam_e = sb("lam_e", [P, 2])
        lam = sb("lam", [P, 2])
        subln = sb("subln", [P, 2])
        subln_s = sb("subln_s", [P, 2])
        wf = sb("wf", [P, DT, 8])
        bf = sb("bf", [P, 8])
        fg = sb("fg", [P, 4, TB, 8])
        cum_col = sb("cum_col", [P, TB, 8])

        acc = ctx.enter_context(nc.psum_tensor("acc", [P, 4, 512], F32))
        work = ctx.enter_context(nc.psum_tensor("work", [P, 4, 512], F32))

        raw_loaded = [sem(f"raw_loaded{i}") for i in range(RAW)]
        const_loaded, gain_loaded, x_loaded = sem("const_loaded"), sem("gain_loaded"), sem("x_loaded")
        hi_ready = sem("hi_ready")
        lo_ready = sem("lo_ready")
        gate_used = sem("gate_used")
        acc_ready = sem("acc_ready")
        x_updated = sem("x_updated")
        xg_hi_ready, xg_ready = sem("xg_hi_ready"), sem("xg_ready")
        squares_ready, square_sum_ready = sem("squares_ready"), sem("square_sum_ready")
        var_ready, mean_ready, r_col_ready = sem("var_ready"), sem("mean_ready"), sem("r_col_ready")
        r_diag_ready, r_row_psum, r_row_ready = sem("r_diag_ready"), sem("r_row_psum"), sem("r_row_ready")
        gu_psum = sem("gu_psum")
        gu_scaled = sem("gu_scaled")
        silu_ready, h_ready, h_hi_ready, h_split = sem("silu_ready"), sem("h_ready"), sem("h_hi_ready"), sem("h_split")
        down_used = sem("down_used")
        out_used = sem("out_used")
        v_psum, v_ready = sem("v_psum"), sem("v_ready")
        qk_psum, qk_ready = sem("qk_psum"), sem("qk_ready")
        rope_in, rope_psum = sem("rope_in"), sem("rope_psum")
        scores_psum = sem("scores_psum")
        scores_ready = sem("scores_ready")
        exp_ready = sem("exp_ready")
        mix_in = sem("mix_in")
        mixed_psum = sem("mixed_psum")
        logw_ready = sem("logw_ready")
        w_ready = sem("w_ready")
        pv_psum = sem("pv_psum")
        osq_ready, ovar_psum, ovar_ready, or_ready, on_ready = (
            sem("osq_ready"), sem("ovar_psum"), sem("ovar_ready"), sem("or_ready"), sem("on_ready"))
        mix_hi_ready, mix_ready = sem("mix_hi_ready"), sem("mix_ready")
        lam_in_ready, lam_psum, lam_exp, lam_ready = sem("lam_prod"), sem("lam_psum"), sem("lam_exp"), sem("lam_ready")
        f_psum, f_ready, f_ln, logf_ready = sem("f_psum"), sem("f_ready"), sem("f_ln"), sem("logf_ready")
        cum_psum, lf_wide_ready, bias_psum, bias_ready = (
            sem("cum_psum"), sem("lf_wide_ready"), sem("bias_psum"), sem("bias_ready"))
        const_ready = sem("const_ready")
        dve_step, act_step = sem("dve_step"), sem("act_step")
        y_ready, stored = sem("y_ready"), sem("stored")

        ones = cst[:, C_ONES:C_ONES + P]
        ident = cst[:, C_IDENT:C_IDENT + P]
        later = cst[:, C_LATER:C_LATER + P]
        cum = cst[:, C_CUM:C_CUM + 2 * P]
        strict_t = cst[:, C_STRICT_T:C_STRICT_T + TRI]
        causal = cst[:, C_CAUSAL:C_CAUSAL + TRI]
        cos = cst[0:ROT, C_COS:C_COS + T]
        sin = cst[0:ROT, C_SIN:C_SIN + T]
        rot = cst[0:ROT, C_ROT:C_ROT + ROT]
        squares = wide[:].rearrange("p a b -> p (a b)")[:, 0:DT * T].rearrange("p (d t) -> p d t", d=DT)
        attn = work[:, 2:4, 0:TRI]
        s_a, s_b, s_c = (scratch[:, i, :].rearrange("p (h c) -> p h c", h=2) for i in range(3))
        head_out = scratch[:, 3, 0:2 * T]
        gu_sb = [scratch[:, i, 0:512].rearrange("p (g t) -> p g t", g=2) for i in range(2)]
        silu_sb = [scratch[:, 2, i * T:(i + 1) * T] for i in range(2)]
        h_sb = [scratch[:, 3, i * T:(i + 1) * T] for i in range(2)]
        lf_wide = scratch[:].rearrange("p a b -> p (a b)")[:, 0:8 * T].rearrange("p (h b n) -> p h b n", h=8, b=TB)
        both = lambda a: a.unsqueeze(1).broadcast_to([a.shape[0], 2, a.shape[1]])
        flat = lambda a: a.rearrange("p a b -> p (a b)")
        halves = lambda ap: ap.rearrange("p (h t) -> p h t", h=2)

        def proj(w, c):
            return w[:, c % RING, :].rearrange("p (k n) -> p k n", k=DT)

        def down(w, c):
            return w[:, c % RING, :].rearrange("p (k n) -> p k n", k=2)

        def acc_tile(d):
            return acc[:, d // 2, (d % 2) * T:(d % 2 + 1) * T]

        def ffn_steps(run, c0):
            def first(s):
                return c0 + max(0, 3 * s - 1)
            run(0, first(0), 0)
            run(1, first(1), 0)
            yield (UNITS - 3) // 2, lambda turn: (run(2, first(2), turn), run(3, first(3), turn))
            run(UNITS - 1, first(UNITS - 1), 0)

        def slot_free(eng, c, turn=0):
            if c < RING:
                return
            c -= RING
            layer, n, c0, att, no = [p for p in phases() if p[2] <= c][-1]
            what, j = (ATT_ORDER if att else FFN_ORDER)[c - c0]
            if (what, j) in (("down", UNITS - 1), ("o", PAIRS - 1)):
                eng.wait_ge(acc_ready, DT * (n + 1))
            elif what == "gate":
                eng.wait_ge(gate_used, no * UNITS + j + 1 + turn * 2)
            elif what == "up":
                eng.wait_ge(gu_psum, no * FFN_TILES + 2 * j + 2 + turn * 4)
            elif what == "down":
                eng.wait_ge(down_used, no * (UNITS - 1) + j + 1 + turn * 2)
            elif what == "v":
                eng.wait_ge(v_psum, layer * PAIRS + j + 1)
            elif what == "o":
                eng.wait_ge(out_used, layer * (PAIRS - 1) + j + 1)
            else:
                eng.wait_ge(qk_psum, 2 * (layer * PAIRS + j) + (what == "k") + 1)

        block = ctx.enter_context(nc.Block())

        @block.sync
        def _(sp):
            def load(c, chunk):
                sp.dma_start(raw[:, c % RAW, :], stream[chunk]).then_inc(raw_loaded[c % RAW], 16)

            sp.dma_start(gain[:], gains).then_inc(gain_loaded, 16)
            sp.dma_start(x[:], x_in).then_inc(x_loaded, 16)
            for c in range(RAW):
                load(c, c)
            for tile, source in ((cst, consts), (lam_q, lam_in), (subln, subln_in), (wf, wf_in), (bf, bf_in)):
                sp.dma_start(tile[:], source).then_inc(const_loaded, 16)
            rounds = CHUNKS // RAW - 1
            with sp.Fori(0, rounds) as turn:
                for k in range(RAW):
                    sp.wait_ge(lo_ready, turn * RAW + (k + 1))
                    load(RAW + k, turn * RAW + (RAW + k))
            for c in range((rounds + 1) * RAW, CHUNKS):
                sp.wait_ge(lo_ready, c - RAW + 1)
                load(c, c)
            for d in range(DT):
                sp.wait_ge(y_ready, d + 1)
                sp.dma_start(out[:, d, :], x[:, d, :]).then_inc(stored, 16)
            sp.wait_ge(stored, 16 * DT)

        @block.gpsimd
        def _(pool):
            nc.gpsimd.memset(half_neg[:], -0.5).then_inc(const_ready, 1)
            pool.wait_ge(const_ready, 1)
            for n in range(NORMS):
                pool.wait_ge(mean_ready, n + 1)
                nc.gpsimd.tensor_tensor(r_col[:], mean[:], half_neg[:], ALU.pow).then_inc(r_col_ready, 1)

        @block.scalar
        def _(act):
            split = [0]
            own = [0]

            def own_step():
                own[0] += 1
                act.wait_ge(act_step, own[0])

            def hi(c, turn=0):
                act.wait_ge(raw_loaded[c % RAW], 16 * (c // RAW + 1) + turn * (16 * RING // RAW))
                slot_free(act, c, turn)
                nc.scalar.activation(w_hi[:, c % RING, :], raw[:, c % RAW, :], ACT.Copy).then_inc(hi_ready, 1)

            def split_to(c):
                while split[0] <= min(c, CHUNKS - 1):
                    hi(split[0])
                    split[0] += 1

            def ffn(layer, n, c0, _, f):
                split_to(c0 + 4)

                def step(s, c, turn):
                    t0 = f * FFN_TILES + 2 * s

                    def split_next(k):
                        if 2 <= s < UNITS - 1:
                            hi(c + 3 + k, turn)
                        else:
                            split_to(c + 3 + k if s else c + 4)

                    for k in range(2):
                        t = t0 + k
                        if k == 0 or s < UNITS - 1:
                            split_next(k)
                        act.wait_ge(gu_scaled, t + 1 + turn * 4)
                        nc.scalar.activation(silu_sb[t % 2], gu_sb[t % 2][:, 0, :], ACT.Silu).then_inc(silu_ready, 1)
                        if k == 1 and s < UNITS - 1:
                            split_next(2)
                        act.wait_ge(h_ready, t + 1 + turn * 4)
                        if k == 0 and s >= 2:
                            act.wait_ge(down_used, f * (UNITS - 1) + s - 1 + turn * 2)
                        nc.scalar.activation(m_hi[:, t % 4, :], h_sb[t % 2], ACT.Copy).then_inc(h_hi_ready, 1)

                for turns, body in ffn_steps(step, c0):
                    with act.Fori(0, turns) as turn:
                        body(turn)
                    split[0] = c0 + 3 * (UNITS - 2) - 1 + RING
                split_to(c0 + FFN_CHUNKS + 2)

            def attention(layer, n, c0, _, kind):
                first = layer * PAIRS
                kind = KINDS[layer]
                for c in range(PAIRS):
                    split_to(c0 + c + 3)
                    act.wait_ge(v_psum, first + c + 1)
                    if c == 0:
                        act.wait_ge(r_col_ready, n + 1)
                    for tb in range(TB):
                        ins = nc.scalar.activation(v[:, tb, c * COLS:(c + 1) * COLS], work[:, c, tb * T:(tb + 1) * T],
                                                   ACT.Identity, scale=r_col[:, tb:tb + 1])
                    ins.then_inc(v_ready, 1)
                if kind == DIFF:
                    act.wait_ge(lam_psum, 1)
                    nc.scalar.activation(lam_e[:], work[:, 3, 0:2], ACT.Exp).then_inc(lam_exp, 1)
                if kind == FOX:
                    act.wait_ge(f_ready, 1)
                    nc.scalar.activation(fg[:, 1], fg[:, 0], ACT.Abs).then_inc(act_step, 1)
                    own_step()
                    nc.scalar.activation(fg[:, 1], fg[:, 1], ACT.Exp, scale=-1.0).then_inc(act_step, 1)
                    own_step()
                    nc.scalar.activation(fg[:, 2], fg[:, 1], ACT.Ln, bias=1.0).then_inc(f_ln, 1)
                def weights(b):
                    if kind == STICK:
                        act.wait_ge(logw_ready, KINDS[:layer].count(STICK) * PAIRS + b - first + 1)
                        nc.scalar.activation(w_t[:], s_b, ACT.Exp).then_inc(w_ready, 1)
                    else:
                        maps = 1 if kind == DIFF else 2
                        act.wait_ge(mixed_psum, b + 1)
                        nc.scalar.activation(w_t[:, 0:maps], attn[:, 0:maps], ACT.Copy).then_inc(w_ready, 1)

                def mix(b):
                    act.wait_ge(pv_psum, b + 1)
                    slot = 2 * (b % 2)
                    if kind != DIFF:
                        nc.scalar.activation(m_hi[:, slot:slot + 2, :], halves(work[:, 0, :]),
                                             ACT.Copy).then_inc(mix_hi_ready, 1)
                        return
                    nc.scalar.activation(head_out, work[:, 0, :], ACT.Copy)
                    nc.scalar.activation(scratch[:, 2, 0:2 * T], work[:, 0, :], ACT.Square).then_inc(osq_ready, 1)

                def sub_norm(b):
                    act.wait_ge(ovar_ready, b - first + 1)
                    nc.scalar.activation(scratch[:, 2, 0:T], scratch[:, 2, 0:T], ACT.Ln).then_inc(act_step, 1)
                    own_step()
                    nc.scalar.activation(scratch[:, 2, 0:T], scratch[:, 2, 0:T], ACT.Exp, scale=-0.5).then_inc(or_ready, 1)

                def sub_norm_split(b):
                    slot = 2 * (b % 2)
                    act.wait_ge(on_ready, b - first + 1)
                    for h in range(2):
                        ins = nc.scalar.activation(m_hi[:, slot + h, :], head_out[:, h * T:(h + 1) * T],
                                                   ACT.Identity, scale=subln_s[:, h:h + 1])
                    ins.then_inc(mix_hi_ready, 1)

                def exponentials(a):
                    act.wait_ge(scores_ready, a + 1)
                    if kind == STICK:
                        nc.scalar.activation(s_b, s_a, ACT.Abs).then_inc(act_step, 1)
                        own_step()
                        nc.scalar.activation(s_b, s_b, ACT.Exp, scale=-1.0).then_inc(act_step, 1)
                        own_step()
                        nc.scalar.activation(s_c, s_b, ACT.Ln, bias=1.0).then_inc(exp_ready, 1)
                    else:
                        for h in range(2):
                            for tb, cols in enumerate(ROWS):
                                ins = nc.scalar.activation(s_b[:, h, cols], s_a[:, h, cols], ACT.Exp,
                                                           bias=neg_max[:, h, tb:tb + 1],
                                                           accum_out=row_sum[:, h, tb:tb + 1])
                        ins.then_inc(exp_ready, 1)

                for j in range(PAIRS + 1):
                    a, b = first + j, first + j - 1
                    if j < PAIRS:
                        q_chunk = c0 + ATT_ORDER.index(("q", j))
                        split_to(q_chunk + 4)
                    if j:
                        weights(b)
                    if j < PAIRS:
                        split_to(q_chunk + 5)
                    if j:
                        mix(b)
                    if j and kind == DIFF:
                        sub_norm(b)
                    if j < PAIRS:
                        exponentials(a)
                    if j and kind == DIFF:
                        sub_norm_split(b)
                split_to(c0 + ATT_CHUNKS + 2)

            def gains_and_squares(n):
                for d in range(DT):
                    if n:
                        act.wait_ge(x_updated, DT * (n - 1) + d + 1)
                    if n < NORMS - 1:
                        nc.scalar.activation(xg_hi[:, d, :], x[:, d, :], ACT.Identity,
                                             scale=gain[:, n, d:d + 1]).then_inc(xg_hi_ready, 1)
                    if d % 2:
                        nc.scalar.activation(squares[:, d - 1:d + 1, :], x[:, d - 1:d + 1, :],
                                             ACT.Square).then_inc(squares_ready, 1)

            act.wait_ge(gain_loaded, 16)
            act.wait_ge(x_loaded, 16)
            gains_and_squares(0)
            for phase in phases():
                (attention if phase[3] else ffn)(*phase)
                gains_and_squares(phase[1] + 1)

        @block.vector
        def _(dve):
            split = [0]
            own = [0]

            def done(ins):
                own[0] += 1
                ins.then_inc(dve_step, 1)
                dve.wait_ge(dve_step, own[0])

            def lo(c, turn=0):
                dve.wait_ge(hi_ready, c + 1 + turn * RING)
                nc.vector.tensor_tensor(w_lo[:, c % RING, :], raw[:, c % RAW, :], w_hi[:, c % RING, :].bitcast(F32),
                                        ALU.subtract).then_inc(lo_ready, 1)

            def split_to(c):
                while split[0] <= min(c, CHUNKS - 1):
                    lo(split[0])
                    split[0] += 1

            def norm_mean(n):
                dve.wait_ge(var_ready, n + 1)
                nc.vector.tensor_scalar(mean[:], acc[:, 0, 0:TB], 1.0 / D, EPS, ALU.mult, ALU.add).then_inc(mean_ready, 1)

            def norm_diag(n):
                if n == 0:
                    dve.wait_ge(const_loaded, 16 * 5)
                dve.wait_ge(r_col_ready, n + 1)
                for tb in range(TB):
                    ins = nc.vector.tensor_scalar(r_diag[:, tb * P:(tb + 1) * P], ident, r_col[:, tb:tb + 1], None,
                                                  ALU.mult)
                ins.then_inc(r_diag_ready, 1)

            def norm_row(n):
                dve.wait_ge(r_row_psum, n + 1)
                nc.vector.tensor_copy(r_row[:], acc[:, 1, 0:T]).then_inc(r_row_ready, 1)

            def ffn(layer, n, c0, _, f):
                split_to(c0 + 2)
                norm_mean(n)
                norm_diag(n)
                split_to(c0 + 3)
                norm_row(n)
                split_to(c0 + 4)
                dve.wait_ge(r_row_ready, n + 1)

                def step(s, c, turn):
                    t0 = f * FFN_TILES + 2 * s

                    def split_next(k):
                        if 2 <= s < UNITS - 1:
                            lo(c + 3 + k, turn)
                        else:
                            split_to(c + 3 + k if s else c + 4)

                    for k in range(2):
                        t = t0 + k
                        dve.wait_ge(gu_psum, t + 1 + turn * 4)
                        nc.vector.tensor_tensor(gu_sb[t % 2], halves(work[:, t % 4, :]), both(r_row[:]),
                                                ALU.mult).then_inc(gu_scaled, 1)
                        if k == 0 or s < UNITS - 1:
                            split_next(2 * k)
                        dve.wait_ge(silu_ready, t + 1 + turn * 4)
                        nc.vector.tensor_tensor(h_sb[t % 2], silu_sb[t % 2], gu_sb[t % 2][:, 1, :],
                                                ALU.mult).then_inc(h_ready, 1)
                        if k == 0 and s < UNITS - 1:
                            split_next(1)
                        dve.wait_ge(h_hi_ready, t + 1 + turn * 4)
                        nc.vector.tensor_tensor(m_lo[:, t % 4, :], h_sb[t % 2], m_hi[:, t % 4, :].bitcast(F32),
                                                ALU.subtract).then_inc(h_split, 1)

                for turns, body in ffn_steps(step, c0):
                    with dve.Fori(0, turns) as turn:
                        body(turn)
                    split[0] = c0 + 3 * (UNITS - 2) - 1 + RING
                split_to(c0 + FFN_CHUNKS + 1)

            def attention(layer, n, c0, _, kind):
                kind = KINDS[layer]
                first = layer * PAIRS
                split_to(c0 + 2)
                norm_mean(n)
                norm_diag(n)
                split_to(c0 + 3)
                norm_row(n)
                split_to(c0 + 4)
                if kind == DIFF:
                    lp = lam_q[:].rearrange("p (a b) -> p a b", b=2)
                    nc.vector.tensor_tensor(lam_p[:], lp[:, :, 0], lp[:, :, 1], ALU.mult).then_inc(lam_in_ready, 1)
                    nc.vector.tensor_scalar(subln_s[:], subln[:], 1.0 - LAM_INIT, None, ALU.mult)
                    dve.wait_ge(lam_exp, 1)
                    done(nc.vector.tensor_tensor(lam[:, 0:1], lam_e[:, 0:1], lam_e[:, 1:2], ALU.subtract))
                    done(nc.vector.tensor_scalar(lam[:, 1:2], lam[:, 0:1], LAM_INIT, None, ALU.add))
                if kind == FOX:
                    dve.wait_ge(f_psum, 1)
                    for tb in range(TB):
                        ins = nc.vector.scalar_tensor_tensor(
                            out=fg[:, 0, tb, :], in0=work[:, 3, tb * 8:(tb + 1) * 8], scalar=r_col[:, tb:tb + 1],
                            in1=bf[:], op0=ALU.mult, op1=ALU.add)
                    ins.then_inc(f_ready, 1)
                    dve.wait_ge(f_ln, 1)
                    nc.vector.scalar_tensor_tensor(out=flat(fg[:, 3]), in0=flat(fg[:, 0]), scalar=0.0,
                                                   in1=flat(fg[:, 2]), op0=ALU.min,
                                                   op1=ALU.subtract).then_inc(logf_ready, 1)
                dve.wait_ge(r_row_ready, n + 1)

                def forget_cums():
                    dve.wait_ge(cum_psum, 1)
                    nc.vector.tensor_copy(flat(cum_col[:]), work[:, 3, 0:2 * 8])
                    for head in range(2 * PAIRS):
                        for tb in range(TB):
                            ins = nc.vector.tensor_scalar(lf_wide[:, head, tb, :], ones, fg[:, 3, tb, head:head + 1],
                                                          None, ALU.mult)
                    ins.then_inc(lf_wide_ready, 1)

                def forget_bias():
                    for pair in range(PAIRS):
                        dve.wait_ge(bias_psum, pair + 1)
                        for h in range(2):
                            bank = work[:, (2 + pair) % 4, h * T:(h + 1) * T]
                            head = 2 * pair + h
                            nc.vector.tensor_tensor(wide[:, head, 0:P], causal[:, 0:P], bank[:, 0:P], ALU.subtract)
                            ins = nc.vector.tensor_tensor(wide[:, head, P:TRI], causal[:, P:TRI], bank, ALU.subtract)
                        ins.then_inc(bias_ready, 1)
                    dve.wait_ge(bias_ready, PAIRS)

                def scale_qk(dst, bank, count, scale):
                    dve.wait_ge(qk_psum, count)
                    nc.vector.scalar_tensor_tensor(out=dst[:], in0=halves(work[:, bank, :]), scalar=scale,
                                                   in1=both(r_row[:]), op0=ALU.mult,
                                                   op1=ALU.mult).then_inc(rope_in if kind == DIFF else qk_ready, 1)

                def rotate(dst, bank, k):
                    turned = wide[0:ROT, 0:2, 0:T]
                    dve.wait_ge(rope_psum, k)
                    nc.vector.tensor_tensor(dst[0:ROT], dst[0:ROT], both(cos), ALU.mult)
                    done(nc.vector.tensor_tensor(turned, halves(work[0:ROT, bank, :]), both(sin), ALU.mult))
                    nc.vector.tensor_tensor(dst[0:ROT], dst[0:ROT], turned, ALU.add).then_inc(qk_ready, 1)

                def log_weights(b):
                    dve.wait_ge(mixed_psum, b + 1)
                    nc.vector.tensor_tensor(s_b, s_a, attn, ALU.subtract).then_inc(logw_ready, 1)

                def mix(b):
                    slot = 2 * (b % 2)
                    dve.wait_ge(mix_hi_ready, b + 1)
                    nc.vector.tensor_tensor(m_lo[:, slot:slot + 2, :], halves(work[:, 0, :]),
                                            m_hi[:, slot:slot + 2, :].bitcast(F32),
                                            ALU.subtract).then_inc(mix_ready, 1)

                def sub_norm_mean(b):
                    dve.wait_ge(ovar_psum, b - first + 1)
                    nc.vector.tensor_scalar(scratch[:, 2, 0:T], work[:, 1, 0:T], 1.0 / COLS, EPS, ALU.mult,
                                            ALU.add).then_inc(ovar_ready, 1)

                def sub_norm(b):
                    dve.wait_ge(or_ready, b - first + 1)
                    nc.vector.tensor_tensor(halves(head_out), halves(head_out), both(scratch[:, 2, 0:T]),
                                            ALU.mult).then_inc(on_ready, 1)

                def sub_norm_split(b):
                    slot = 2 * (b % 2)
                    dve.wait_ge(mix_hi_ready, b + 1)
                    for h in range(2):
                        ins = nc.vector.scalar_tensor_tensor(
                            out=m_lo[:, slot + h, :], in0=head_out[:, h * T:(h + 1) * T],
                            scalar=subln_s[:, h:h + 1], in1=m_hi[:, slot + h, :].bitcast(F32),
                            op0=ALU.mult, op1=ALU.subtract)
                    ins.then_inc(mix_ready, 1)

                def mask(a):
                    j = a - first
                    dve.wait_ge(scores_psum, a + 1)
                    if kind == STICK:
                        nc.vector.tensor_tensor(s_a, attn, both(strict_t), ALU.add).then_inc(scores_ready, 1)
                        return
                    if kind == DIFF:
                        done(nc.vector.tensor_tensor(s_a, attn, both(causal), ALU.add))
                    else:
                        for h in range(2):
                            for tb, cols in enumerate(ROWS):
                                ins = nc.vector.scalar_tensor_tensor(
                                    out=s_a[:, h, cols], in0=attn[:, h, cols], scalar=cum_col[:, tb, 2 * j + h:2 * j + h + 1],
                                    in1=wide[:, 2 * j + h, cols], op0=ALU.add, op1=ALU.add)
                        done(ins)
                    for tb, cols in enumerate(ROWS):
                        ins = nc.vector.tensor_reduce(row_max[:, :, tb], s_a[:, :, cols], AX_X, ALU.max)
                    done(ins)
                    nc.vector.tensor_scalar(neg_max[:], row_max[:], -1.0, None, ALU.mult).then_inc(scores_ready, 1)

                def normalise(a):
                    dve.wait_ge(exp_ready, a + 1)
                    if kind == STICK:
                        nc.vector.scalar_tensor_tensor(out=s_c, in0=s_a, scalar=0.0, in1=s_c, op0=ALU.max,
                                                       op1=ALU.add).then_inc(mix_in, 1)
                        return
                    done(nc.vector.reciprocal(row_inv[:], row_sum[:]))
                    if kind == FOX:
                        for h in range(2):
                            for tb, cols in enumerate(ROWS):
                                ins = nc.vector.tensor_scalar(s_a[:, h, cols], s_b[:, h, cols],
                                                              row_inv[:, h, tb:tb + 1], None, ALU.mult)
                        ins.then_inc(mix_in, 1)
                        return
                    for tb, cols in enumerate(ROWS):
                        ins = nc.vector.tensor_scalar(s_a[:, 1, cols], s_b[:, 1, cols], row_inv[:, 1, tb:tb + 1],
                                                      lam[:, 1:2], ALU.mult, ALU.mult)
                    done(ins)
                    for tb, cols in enumerate(ROWS):
                        ins = nc.vector.scalar_tensor_tensor(
                            out=s_a[:, 0, cols], in0=s_b[:, 0, cols], scalar=row_inv[:, 0, tb:tb + 1],
                            in1=s_a[:, 1, cols], op0=ALU.mult, op1=ALU.subtract)
                    ins.then_inc(mix_in, 1)

                for j in range(PAIRS + 1):
                    a, b = first + j, first + j - 1
                    if j < PAIRS:
                        q_chunk = c0 + ATT_ORDER.index(("q", j))
                        split_to(q_chunk + 3)
                        if kind == FOX and j == 0:
                            forget_cums()
                        scale_qk(q_t, 0, 2 * a + 1, SCALE)
                        split_to(q_chunk + 4)
                        if kind == DIFF:
                            rotate(q_t, 0, 2 * j + 1)
                    if j and kind == STICK:
                        log_weights(b)
                    if j < PAIRS:
                        scale_qk(k_t, 1, 2 * a + 2, 1.0)
                        if kind == DIFF:
                            rotate(k_t, 1, 2 * j + 2)
                        if kind == FOX and j == 0:
                            forget_bias()
                    if j and kind != DIFF:
                        mix(b)
                    if j and kind == DIFF:
                        sub_norm_mean(b)
                    if j < PAIRS:
                        mask(a)
                        if kind != DIFF:
                            split_to(q_chunk + 5)
                    if j and kind == DIFF:
                        sub_norm(b)
                    if j < PAIRS:
                        normalise(a)
                    if j and kind == DIFF:
                        sub_norm_split(b)
                    if j < PAIRS:
                        split_to(q_chunk + 5)
                split_to(c0 + ATT_CHUNKS + 1)

            def update(n, scale):
                for d in range(DT + 1):
                    if d < DT and n:
                        if d % 2 == 0:
                            dve.wait_ge(acc_ready, DT * (n - 1) + d + 2)
                        nc.vector.scalar_tensor_tensor(out=x[:, d, :], in0=acc_tile(d), scalar=scale, in1=x[:, d, :],
                                                       op0=ALU.mult, op1=ALU.add).then_inc(x_updated, 1)
                    if d and n < NORMS - 1:
                        dve.wait_ge(xg_hi_ready, DT * n + d)
                        nc.vector.scalar_tensor_tensor(
                            out=xg_lo[:, d - 1, :], in0=x[:, d - 1, :], scalar=gain[:, n, d - 1:d],
                            in1=xg_hi[:, d - 1, :].bitcast(F32), op0=ALU.mult, op1=ALU.subtract).then_inc(xg_ready, 1)
                    if d >= 5 and d % 2 or d == DT:
                        at = d - 3 if d < DT else DT - 2
                        dve.wait_ge(squares_ready, n * DT // 2 + at // 2 + 1)
                        done(nc.vector.tensor_tensor(squares[:, 0:2, :], squares[:, 0:2, :],
                                                     squares[:, at:at + 2, :], ALU.add))
                nc.vector.tensor_tensor(squares[:, 0, :], squares[:, 0, :], squares[:, 1, :],
                                        ALU.add).then_inc(square_sum_ready, 1)

            dve.wait_ge(gain_loaded, 16)
            dve.wait_ge(x_loaded, 16)
            update(0, 1.0)
            for phase in phases():
                (attention if phase[3] else ffn)(*phase)
                update(phase[1] + 1, 1.0 if phase[3] else 0.5)

            n = NORMS - 1
            norm_mean(n)
            norm_diag(n)
            norm_row(n)
            dve.wait_ge(r_row_ready, n + 1)
            for d in range(DT):
                nc.vector.scalar_tensor_tensor(out=x[:, d, :], in0=x[:, d, :], scalar=gain[:, n, d:d + 1],
                                               in1=r_row[:], op0=ALU.mult, op1=ALU.mult).then_inc(y_ready, 1)

        @block.tensor
        def _(pe):
            def product(dst, a_hi, a_lo, b_hi, b_lo, start, stop, skip=False):
                nc.tensor.matmul(dst, a_hi, b_hi, start=start, stop=False, skip_group_check=skip)
                nc.tensor.matmul(dst, a_hi, b_lo, start=False, stop=False, skip_group_check=skip)
                return nc.tensor.matmul(dst, a_lo, b_hi, start=False, stop=stop, skip_group_check=skip)

            def project(dst, c, col):
                for k in range(DT):
                    ins = product(dst, proj(w_hi, c)[:, k, col:col + P], proj(w_lo, c)[:, k, col:col + P],
                                  xg_hi[:, k, :], xg_lo[:, k, :], start=k == 0, stop=k == DT - 1)
                return ins

            def contract_pair(c, slot, first, last):
                for d, t in [(d, t) for bank in range(0, DT, 2) for t in range(2) for d in (bank, bank + 1)]:
                    ins = product(acc_tile(d), down(w_hi, c)[:, t, d * P:(d + 1) * P],
                                  down(w_lo, c)[:, t, d * P:(d + 1) * P], m_hi[:, slot + t, :], m_lo[:, slot + t, :],
                                  start=first and t == 0 and d % 2 == 0, stop=last and t == 1, skip=True)
                    if last and t == 1:
                        ins.then_inc(acc_ready, 1)
                return ins

            def norm_var(n):
                if n == 0:
                    pe.wait_ge(const_loaded, 16 * 5)
                pe.wait_ge(square_sum_ready, n + 1)
                for tb in range(TB):
                    ins = nc.tensor.matmul(acc[:, 0, tb:tb + 1], squares[:, 0, tb * P:(tb + 1) * P], ones[:, 0:1],
                                           start=True, stop=True)
                ins.then_inc(var_ready, 1)

            def norm_row(n):
                pe.wait_ge(r_diag_ready, n + 1)
                nc.tensor.matmul(acc[:, 1, 0:T], ones, r_diag[:], start=True, stop=True).then_inc(r_row_psum, 1)

            def ffn(layer, n, c0, _, f):
                def first_step():
                    for parts in (((0,), (1,)) if n == 0 else ((0, 1),)):
                        pe.wait_ge(lo_ready, c0 + parts[-1] + 1)
                        for k in range(DT):
                            if parts[0] == 0:
                                pe.wait_ge(xg_ready, DT * n + k + 1)
                            for part in parts:
                                for i in range(2):
                                    t = f * FFN_TILES + i
                                    ins = product(work[:, t % 4, part * T:(part + 1) * T],
                                                  proj(w_hi, c0 + part)[:, k, i * P:(i + 1) * P],
                                                  proj(w_lo, c0 + part)[:, k, i * P:(i + 1) * P],
                                                  xg_hi[:, k, :], xg_lo[:, k, :],
                                                  start=k == 0 and part == 0, stop=k == DT - 1, skip=True)
                                    if k == DT - 1 and part:
                                        ins.then_inc(gu_psum, 1)
                                    elif k == DT - 1 and i:
                                        ins.then_inc(gate_used, 1)
                            if k == NORM_AT and parts[-1] == 1:
                                norm_var(n)
                    norm_row(n)

                def step(s, c, turn):
                    if s == 0:
                        first_step()
                        return
                    pe.wait_ge(lo_ready, c + 2 + turn * RING)
                    for k in range(2):
                        t = f * FFN_TILES + 2 * s + k
                        if s >= 2:
                            pe.wait_ge(gu_scaled, t - 3 + turn * 4)
                        ins = project(work[:, t % 4, 0:T], c, k * P)
                        if k == 1:
                            ins.then_inc(gate_used, 1)
                        project(work[:, t % 4, T:2 * T], c + 1, k * P).then_inc(gu_psum, 1)
                    unit_down(s - 1, c + 2, turn).then_inc(down_used, 1)

                def unit_down(u, c, turn, last=False):
                    pe.wait_ge(lo_ready, c + 1 + turn * RING)
                    pe.wait_ge(h_split, f * FFN_TILES + 2 * u + 2 + turn * 4)
                    return contract_pair(c, (f * FFN_TILES + 2 * u) % 4, u == 0, last)

                for turns, body in ffn_steps(step, c0):
                    with pe.Fori(0, turns) as turn:
                        body(turn)
                unit_down(UNITS - 1, c0 + FFN_CHUNKS - 1, 0, True)

            def attention(layer, n, c0, _, kind):
                kind = KINDS[layer]
                first = layer * PAIRS

                for chunks in ((0, 1), (2,), (3,)):
                    pe.wait_ge(lo_ready, c0 + chunks[-1] + 1)
                    for k in range(DT):
                        if chunks[0] == 0:
                            pe.wait_ge(xg_ready, DT * n + k + 1)
                        for c in chunks:
                            for tb in range(TB):
                                ins = product(work[:, c, tb * T:(tb + 1) * T], xg_hi[:, k, tb * P:(tb + 1) * P],
                                              xg_lo[:, k, tb * P:(tb + 1) * P], proj(w_hi, c0 + c)[:, k, :],
                                              proj(w_lo, c0 + c)[:, k, :],
                                              start=k == 0 and tb == 0, stop=k == DT - 1, skip=True)
                            if k == DT - 1:
                                ins.then_inc(v_psum, 1)
                        if chunks[0] == 0 and k == NORM_AT:
                            norm_var(n)
                    if chunks[0] == 0:
                        norm_row(n)
                pe.wait_ge(v_ready, first + PAIRS)
                if kind == DIFF:
                    pe.wait_ge(lam_in_ready, 1)
                    nc.tensor.matmul(work[:, 3, 0:2], ones, lam_p[:], start=True, stop=True).then_inc(lam_psum, 1)
                if kind == FOX:
                    for tb in range(TB):
                        for k in range(DT):
                            for part in (xg_hi, xg_lo):
                                ins = nc.tensor.matmul(
                                    work[:, 3, tb * 8:(tb + 1) * 8], part[:, k, tb * P:(tb + 1) * P].bitcast(F32),
                                    wf[:, k, :], start=k == 0 and part is xg_hi, stop=k == DT - 1 and part is xg_lo)
                    ins.then_inc(f_psum, 1)

                def head_projection(c, bank, h):
                    pe.wait_ge(lo_ready, c + 1)
                    ins = project(work[:, bank, h * T:(h + 1) * T], c, h * P)
                    if h:
                        ins.then_inc(qk_psum, 1)

                def rotate(t, bank, j, k):
                    pe.wait_ge(rope_in, 2 * j + k)
                    nc.tensor.matmul(work[0:ROT, bank, :], rot, flat(t[0:ROT]), start=True,
                                     stop=True).then_inc(rope_psum, 1)

                def forget_cums():
                    pe.wait_ge(logf_ready, 1)
                    nc.tensor.matmul(work[:, 3, 0:8], cum[:, 0:P], fg[:, 3, 0, :], start=True, stop=True)
                    nc.tensor.matmul(work[:, 3, 8:16], ones, fg[:, 3, 0, :], start=True, stop=False)
                    nc.tensor.matmul(work[:, 3, 8:16], cum[:, 0:P], fg[:, 3, 1, :], start=False,
                                     stop=True).then_inc(cum_psum, 1)

                def forget_bias():
                    pe.wait_ge(lf_wide_ready, 1)
                    for pair in range(PAIRS):
                        if pair >= 2:
                            pe.wait_ge(qk_ready, 2 * first + pair - 1)
                        for h in range(2):
                            bank, head = work[:, (2 + pair) % 4, h * T:(h + 1) * T], 2 * pair + h
                            nc.tensor.matmul(bank, lf_wide[:, head, 0, :], cum, start=True, stop=True)
                            ins = nc.tensor.matmul(bank[:, P:T], lf_wide[:, head, 1, :], cum[:, 0:P], start=False,
                                                   stop=True, skip_group_check=True)
                        ins.then_inc(bias_psum, 1)
                    pe.wait_ge(bias_ready, 2)

                def scores(a):
                    pe.wait_ge(qk_ready, 2 * a + 2)
                    for h in range(2):
                        q, k, bank = q_t[:, h, :], k_t[:, h, :], work[:, 2 + h, :]
                        if kind == STICK:
                            nc.tensor.matmul(bank[:, 0:T], k[:, 0:P], q, start=True, stop=True)
                            ins = nc.tensor.matmul(bank[:, T:TRI], k[:, P:T], q[:, P:T], start=True, stop=True)
                        else:
                            nc.tensor.matmul(bank[:, 0:P], q[:, 0:P], k[:, 0:P], start=True, stop=True)
                            ins = nc.tensor.matmul(bank[:, P:TRI], q[:, P:T], k, start=True, stop=True)
                    ins.then_inc(scores_psum, 1)

                def mixed(b):
                    pe.wait_ge(mix_in, b + 1)
                    for h in range(1 if kind == DIFF else 2):
                        bank = work[:, 2 + h, :]
                        if kind == STICK:
                            nc.tensor.matmul(bank[:, 0:TRI], later, s_c[:, h, :], start=True, stop=True)
                            ins = nc.tensor.matmul(bank[:, P:T], ones, s_c[:, h, T:TRI], start=False, stop=True,
                                                   skip_group_check=True)
                        else:
                            for at in range(0, TRI, P):
                                ins = nc.tensor.transpose(bank[:, at:at + P], s_a[:, h, at:at + P], ident)
                    ins.then_inc(mixed_psum, 1)

                def weighted_values(b):
                    pe.wait_ge(w_ready, b + 1)
                    for h in range(2):
                        bank, cols = work[:, 0, h * T:(h + 1) * T], slice((2 * (b - first) + h) * HD, (2 * (b - first) + h + 1) * HD)
                        w = w_t[:, 0 if kind == DIFF else h, :]
                        nc.tensor.matmul(bank, v[:, 0, cols], w[:, 0:T], start=True, stop=True)
                        ins = nc.tensor.matmul(bank[:, P:T], v[:, 1, cols], w[:, T:TRI], start=False, stop=True,
                                               skip_group_check=True)
                    ins.then_inc(pv_psum, 1)

                def output_squares(j):
                    pe.wait_ge(osq_ready, j)
                    nc.tensor.matmul(work[:, 1, 0:T], ones, scratch[:, 2, 0:T], start=True, stop=False)
                    nc.tensor.matmul(work[:, 1, 0:T], ones, scratch[:, 2, T:2 * T], start=False,
                                     stop=True).then_inc(ovar_psum, 1)

                def output(j):
                    c, b = c0 + ATT_ORDER.index(("o", j)), first + j
                    pe.wait_ge(lo_ready, c + 1)
                    pe.wait_ge(mix_ready, b + 1)
                    ins = contract_pair(c, 2 * (b % 2), j == 0, j == PAIRS - 1)
                    if j < PAIRS - 1:
                        ins.then_inc(out_used, 1)

                for j in range(PAIRS):
                    a, b = first + j, first + j - 1
                    c = c0 + ATT_ORDER.index(("q", j))
                    if j >= 2:
                        pe.wait_ge(osq_ready, j - 1) if kind == DIFF else pe.wait_ge(mix_ready, b)
                    if kind == FOX and j == 1:
                        pe.wait_ge(bias_ready, PAIRS)
                    head_projection(c, 0, 0)
                    if kind == FOX and j == 0:
                        forget_cums()
                    head_projection(c, 0, 1)
                    if kind == DIFF and j >= 2:
                        pe.wait_ge(ovar_ready, j - 1)
                    head_projection(c + 1, 1, 0)
                    if kind == DIFF:
                        rotate(q_t, 0, j, 1)
                    if j:
                        mixed(b)
                    head_projection(c + 1, 1, 1)
                    if kind == FOX and j == 0:
                        forget_bias()
                    if j:
                        pe.wait_ge(qk_ready, 2 * a + 1)
                        weighted_values(b)
                    if kind == DIFF:
                        rotate(k_t, 1, j, 2)
                    if j >= 2 and (kind == DIFF or j < PAIRS - 1):
                        output(j - 2)
                    if j and kind == DIFF:
                        pe.wait_ge(qk_ready, 2 * a + 2)
                        output_squares(j)
                    scores(a)
                    if j == PAIRS - 1:
                        output(PAIRS - 2 if kind == DIFF else j - 2)
                if kind != DIFF:
                    mixed(first + PAIRS - 1)
                    output(PAIRS - 2)
                else:
                    mixed(first + PAIRS - 1)
                weighted_values(first + PAIRS - 1)
                if kind == DIFF:
                    output_squares(PAIRS)
                output(PAIRS - 1)

            for phase in phases():
                (attention if phase[3] else ffn)(*phase)
            norm_var(NORMS - 1)
            norm_row(NORMS - 1)


def kernel(x, norm_g, final_g, ffn_w_gate, ffn_w_up, ffn_w_down, w_qkv, w_o,
           diff_lambda, diff_subln_g, fox_w_f, fox_b_f):
    import concourse.bacc as bacc
    from concourse.bass_utils import run_bass_kernel_spmd

    a = [np.asarray(w) for w in (ffn_w_gate, ffn_w_up, ffn_w_down, w_qkv, w_o)]
    gate, up, down_w, qkv, w_out = a
    stream = np.empty((CHUNKS, P, CHUNK), np.float32)
    columns = lambda w, u: w[:, u * COLS:(u + 1) * COLS].reshape(DT, P, COLS).transpose(1, 0, 2).reshape(P, CHUNK)
    rows = lambda w, u: w[u * 2 * P:(u + 1) * 2 * P].reshape(2, P, D).transpose(1, 0, 2).reshape(P, CHUNK)
    chunks = []
    for layer in range(DEPTH):
        for part in range(3):
            if part == 1:
                w = qkv[layer]
                cut = {"q": w[:, :D], "k": w[:, D:2 * D], "v": w[:, 2 * D:]}
                chunks += [rows(w_out[layer], j) if what == "o" else columns(cut[what], j) for what, j in ATT_ORDER]
            else:
                cut = {"gate": gate[layer, part // 2], "up": up[layer, part // 2]}
                chunks += [rows(down_w[layer, part // 2], u) if what == "down" else columns(cut[what], u)
                           for what, u in FFN_ORDER]
    for c, chunk in enumerate(chunks):
        stream[c] = chunk
    tiles = lambda t: np.ascontiguousarray(np.asarray(t).reshape(DT, P, -1).transpose(1, 0, 2))
    gains = np.concatenate([np.asarray(norm_g).reshape(3 * DEPTH, D), np.asarray(final_g).reshape(1, D)])
    arrays = {
        "stream": stream,
        "x": tiles(np.asarray(x)[0].T),
        "gains": np.ascontiguousarray(gains.reshape(NORMS, DT, P).transpose(2, 0, 1)),
        "consts": constants(),
        "lam": np.ascontiguousarray(np.asarray(diff_lambda)[0].T),
        "subln": np.ascontiguousarray(np.asarray(diff_subln_g)[0].reshape(2, P).T),
        "wf": tiles(np.asarray(fox_w_f)[0]),
        "bf": np.ascontiguousarray(np.broadcast_to(np.asarray(fox_b_f)[0], (P, 8))),
    }
    nc = bacc.Bacc("TRN2", target_bir_lowering=False, num_devices=1)
    args = [nc.dram_tensor(f"{name}_dram", arr.shape, F32, kind="ExternalInput").ap() for name, arr in arrays.items()]
    out = nc.dram_tensor("out_dram", (P, DT, T), F32, kind="ExternalOutput").ap()
    trunk(nc, *args, out)
    y = run_bass_kernel_spmd(nc, [{f"{name}_dram": arr for name, arr in arrays.items()}], core_ids=[0]).results[0]["out_dram"]
    return np.ascontiguousarray(y.transpose(2, 1, 0).reshape(1, T, D))
```

```python
import math
from contextlib import ExitStack

import numpy as np

import concourse.bass as bass
from concourse import mybir

F32 = mybir.dt.float32
F32R = mybir.dt.float32r
ALU = mybir.AluOpType
ACT = mybir.ActivationFunctionType
AX_X = mybir.AxisListType.X

P = 128
D, T, FF, DEPTH = 1024, 256, 2816, 4
HD = 128
DT = D // P
TB = T // P
COLS = 256
CHUNK = DT * COLS
HALF = CHUNK // 2
UNITS = FF // COLS
PAIRS = D // COLS
FFN_CHUNKS = 3 * UNITS
ATT_CHUNKS = 4 * PAIRS
CHUNKS = DEPTH * (2 * FFN_CHUNKS + ATT_CHUNKS)
FFN_TILES = 2 * UNITS
NORMS = 3 * DEPTH + 1
V_BANK = 2, 3, 2, 0
NORM_AT = 5
PEELED = 4
RAW = 3
RING = 6
SCALE = HD ** -0.5
EPS = 1e-6
NEG = -1e30
TRI = T + P
ROWS = slice(0, P), slice(P, TRI)
STICK, DIFF, FOX = range(3)
KINDS = [i % 3 for i in range(DEPTH)]
ROT = 32
LAM_INIT = 0.8 - 0.6 * math.exp(-0.3 * KINDS.index(DIFF))

C_ONES, C_IDENT, C_LATER, C_CUM = 0, 128, 256, 384
C_STRICT_T, C_CAUSAL, C_COS, C_SIN, C_ROT = 640, 1024, 1408, 1664, 1920
C_END = 1952


ATT_ORDER = ([("v", 0), ("v", 1), ("q", 0), ("k", 0), ("v", 2), ("v", 3), ("q", 1), ("k", 1)]
             + [x for j in range(2, PAIRS) for x in (("q", j), ("k", j), ("o", j - 2))]
             + [("o", PAIRS - 2), ("o", PAIRS - 1)])
FFN_ORDER = ([("gate", 0), ("up", 0)] + [x for u in range(1, UNITS) for x in (("gate", u), ("up", u), ("down", u - 1))]
             + [("down", UNITS - 1)])


def constants():
    c = np.zeros((P, C_END), np.float32)
    a = np.arange(P)
    c[:, C_ONES:C_ONES + P] = 1.0
    c[:, C_IDENT:C_IDENT + P] = np.eye(P)
    c[:, C_LATER:C_LATER + P] = a[:, None] >= a[None, :]
    c[:, C_CUM:C_CUM + P] = a[:, None] <= a[None, :]
    c[:, C_CUM + P:C_CUM + 2 * P] = 1.0
    strict = np.where(a[:, None] < a[None, :], 0.0, NEG)
    causal = np.where(a[None, :] <= a[:, None], 0.0, NEG)
    for at, mask in ((C_STRICT_T, strict), (C_CAUSAL, causal)):
        c[:, at:at + P] = mask
        c[:, at + 2 * P:at + 3 * P] = mask
    half = ROT // 2
    inv = np.float32(500000.0) ** (-np.arange(half, dtype=np.float32) * np.float32(2.0) / np.float32(ROT))
    ang = (np.arange(T, dtype=np.float32)[:, None] * inv[None, :].astype(np.float32)).astype(np.float64).T
    for at, f in ((C_COS, np.cos), (C_SIN, np.sin)):
        c[0:half, at:at + T] = f(ang)
        c[half:ROT, at:at + T] = f(ang)
    for m in range(half):
        c[m + half, C_ROT + m] = -1.0
        c[m, C_ROT + m + half] = 1.0
    return c


def phases():
    out, chunk, ffn = [], 0, 0
    for layer in range(DEPTH):
        for part in range(3):
            att = part == 1
            out.append((layer, 3 * layer + part, chunk, att, layer if att else ffn))
            chunk += ATT_CHUNKS if att else FFN_CHUNKS
            ffn += not att
    return out


def trunk(nc, stream, x_in, gains, consts, lam_in, subln_in, wf_in, bf_in, out):
    with ExitStack() as ctx:
        def sb(name, shape, dt=F32):
            return ctx.enter_context(nc.sbuf_tensor(name, shape, dt))

        def sem(name):
            return ctx.enter_context(nc.semaphore(name))

        raw = sb("raw", [P, RAW, CHUNK])
        w_hi = sb("w_hi", [P, RING, CHUNK], F32R)
        w_lo = sb("w_lo", [P, RING, CHUNK], F32R)
        x = sb("x", [P, DT, T])
        xg_hi = sb("xg_hi", [P, DT, T], F32R)
        xg_lo = sb("xg_lo", [P, DT, T], F32R)
        m_hi = sb("m_hi", [P, 4, T], F32R)
        m_lo = sb("m_lo", [P, 4, T], F32R)
        scratch = sb("scratch", [P, 4, 2 * TRI])
        wide = sb("wide", [P, DT, TRI])
        v = sb("v", [P, TB, D])
        q_t = sb("q_t", [P, 2, T])
        k_t = sb("k_t", [P, 2, T])
        w_t = sb("w_t", [P, 2, TRI])
        cst = sb("cst", [P, C_END])
        gain = sb("gain", [P, NORMS, DT])
        r_row = sb("r_row", [P, T])
        r_diag = sb("r_diag", [P, T])
        mean = sb("mean", [P, TB])
        r_col = sb("r_col", [P, TB])
        half_neg = sb("half_neg", [P, TB])
        warm = sb("warm", [P, 1])
        row_max = sb("row_max", [P, 2, TB])
        neg_max = sb("neg_max", [P, 2, TB])
        row_sum = sb("row_sum", [P, 2, TB])
        row_inv = sb("row_inv", [P, 2, TB])
        lam_q = sb("lam_q", [P, 4])
        lam_p = sb("lam_p", [P, 2])
        lam_e = sb("lam_e", [P, 2])
        lam = sb("lam", [P, 2])
        subln = sb("subln", [P, 2])
        subln_s = sb("subln_s", [P, 2])
        wf = sb("wf", [P, DT, 8])
        bf = sb("bf", [P, 8])
        fg = sb("fg", [P, 4, TB, 8])
        cum_col = sb("cum_col", [P, TB, 8])

        acc = ctx.enter_context(nc.psum_tensor("acc", [P, 4, 512], F32))
        work = ctx.enter_context(nc.psum_tensor("work", [P, 4, 512], F32))

        raw_loaded = [sem(f"raw_loaded{i}") for i in range(RAW)]
        ones_loaded, const_loaded, gain_loaded = sem("ones_loaded"), sem("const_loaded"), sem("gain_loaded")
        x_loaded = sem("x_loaded0"), sem("x_loaded1")
        hi_ready = sem("hi_ready")
        lo_ready = sem("lo_ready")
        gate_used = sem("gate_used")
        acc_ready = sem("acc_ready")
        x_updated = sem("x_updated")
        xg_hi_ready, xg_ready = sem("xg_hi_ready"), sem("xg_ready")
        squares_ready, square_sum_ready = sem("squares_ready"), sem("square_sum_ready")
        var_ready, mean_ready, r_col_ready = sem("var_ready"), sem("mean_ready"), sem("r_col_ready")
        r_diag_ready, r_row_psum, r_row_ready = sem("r_diag_ready"), sem("r_row_psum"), sem("r_row_ready")
        gu_psum = sem("gu_psum")
        gu_scaled = sem("gu_scaled")
        silu_ready, h_ready, h_hi_ready, h_split = sem("silu_ready"), sem("h_ready"), sem("h_hi_ready"), sem("h_split")
        down_used = sem("down_used")
        out_used = sem("out_used")
        v_psum, v_ready = sem("v_psum"), sem("v_ready")
        qk_psum, qk_ready = sem("qk_psum"), sem("qk_ready")
        rope_in, rope_psum = sem("rope_in"), sem("rope_psum")
        scores_psum = sem("scores_psum")
        scores_ready = sem("scores_ready")
        exp_ready = sem("exp_ready")
        mix_in = sem("mix_in")
        mixed_psum = sem("mixed_psum")
        logw_ready = sem("logw_ready")
        w_ready = sem("w_ready")
        pv_psum = sem("pv_psum")
        raw_half_loaded = sem("raw_half_loaded")
        hi_half_ready, lo_half_ready = sem("hi_half_ready"), sem("lo_half_ready")
        osq_ready, ovar_psum, ovar_ready, or_ready, on_ready = (
            sem("osq_ready"), sem("ovar_psum"), sem("ovar_ready"), sem("or_ready"), sem("on_ready"))
        mix_hi_ready, mix_ready = sem("mix_hi_ready"), sem("mix_ready")
        lam_in_ready, lam_psum, lam_exp = sem("lam_in_ready"), sem("lam_psum"), sem("lam_exp")
        f_psum, f_ready, f_ln, logf_ready = sem("f_psum"), sem("f_ready"), sem("f_ln"), sem("logf_ready")
        cum_psum, lf_wide_ready, bias_psum, bias_ready = (
            sem("cum_psum"), sem("lf_wide_ready"), sem("bias_psum"), sem("bias_ready"))
        const_ready = sem("const_ready")
        dve_step, act_step = sem("dve_step"), sem("act_step")
        y_ready, stored = sem("y_ready"), sem("stored")

        ones = cst[:, C_ONES:C_ONES + P]
        ident = cst[:, C_IDENT:C_IDENT + P]
        later = cst[:, C_LATER:C_LATER + P]
        cum = cst[:, C_CUM:C_CUM + 2 * P]
        strict_t = cst[:, C_STRICT_T:C_STRICT_T + TRI]
        causal = cst[:, C_CAUSAL:C_CAUSAL + TRI]
        cos = cst[0:ROT, C_COS:C_COS + T]
        sin = cst[0:ROT, C_SIN:C_SIN + T]
        rot = cst[0:ROT, C_ROT:C_ROT + ROT]
        squares = wide[:].rearrange("p a b -> p (a b)")[:, 0:DT * T].rearrange("p (d t) -> p d t", d=DT)
        attn = work[:, 2:4, 0:TRI]
        s_a, s_b, s_c = (scratch[:, i, :].rearrange("p (h c) -> p h c", h=2) for i in range(3))
        head_out = scratch[:, 3, 0:2 * T]
        gu_sb = [scratch[:, i, 0:512].rearrange("p (g t) -> p g t", g=2) for i in range(2)]
        silu_sb = [scratch[:, 2, i * T:(i + 1) * T] for i in range(2)]
        h_sb = [scratch[:, 3, i * T:(i + 1) * T] for i in range(2)]
        lf_wide = scratch[:].rearrange("p a b -> p (a b)")[:, 0:8 * T].rearrange("p (h b n) -> p h b n", h=8, b=TB)
        both = lambda a: a.unsqueeze(1).broadcast_to([a.shape[0], 2, a.shape[1]])
        flat = lambda a: a.rearrange("p a b -> p (a b)")
        halves = lambda ap: ap.rearrange("p (h t) -> p h t", h=2)

        def proj(w, c):
            return w[:, c % RING, :].rearrange("p (k n) -> p k n", k=DT)

        def down(w, c):
            return w[:, c % RING, :].rearrange("p (k n) -> p k n", k=2)

        def acc_tile(d):
            return acc[:, d // 2, (d % 2) * T:(d % 2 + 1) * T]

        def ffn_steps(run, c0):
            def first(s):
                return c0 + max(0, 3 * s - 1)
            run(0, first(0), 0)
            run(1, first(1), 0)
            yield (UNITS - 3) // 2, lambda turn: (run(2, first(2), turn), run(3, first(3), turn))
            run(UNITS - 1, first(UNITS - 1), 0)

        def slot_free(eng, c, turn=0):
            if c < RING:
                return
            c -= RING
            layer, n, c0, att, no = [p for p in phases() if p[2] <= c][-1]
            what, j = (ATT_ORDER if att else FFN_ORDER)[c - c0]
            if (what, j) in (("down", UNITS - 1), ("o", PAIRS - 1)):
                eng.wait_ge(acc_ready, DT * (n + 1))
            elif what == "gate":
                eng.wait_ge(gate_used, no * UNITS + j + 1 + turn * 2)
            elif what == "up":
                eng.wait_ge(gu_psum, no * FFN_TILES + 2 * j + 2 + turn * 4)
            elif what == "down":
                eng.wait_ge(down_used, no * (UNITS - 1) + j + 1 + turn * 2)
            elif what == "v":
                eng.wait_ge(v_psum, layer * PAIRS + j + 1)
            elif what == "o":
                eng.wait_ge(out_used, layer * (PAIRS - 1) + j + 1)
            else:
                eng.wait_ge(qk_psum, 2 * (layer * PAIRS + j) + (what == "k") + 1)

        block = ctx.enter_context(nc.Block())

        @block.sync
        def _(sp):
            def load(c, chunk):
                sp.dma_start(raw[:, c % RAW, :], stream[chunk]).then_inc(raw_loaded[c % RAW], 16)

            sp.dma_start(gain[:], gains).then_inc(gain_loaded, 16)
            for half in range(2):
                tiles = slice(half * DT // 2, (half + 1) * DT // 2)
                sp.dma_start(x[:, tiles, :], x_in[:, tiles, :]).then_inc(x_loaded[half], 16)
                part = slice(half * HALF, (half + 1) * HALF)
                loaded = raw_loaded[0] if half else raw_half_loaded
                sp.dma_start(raw[:, 0, part], stream[0, :, part]).then_inc(loaded, 16)
            for c in range(1, RAW):
                load(c, c)
            sp.dma_start(cst[:, 0:C_LATER], consts[:, 0:C_LATER]).then_inc(ones_loaded, 16)
            for c in range(RAW, PEELED * RAW):
                sp.wait_ge(lo_ready, c - RAW + 1)
                load(c, c)
            for tile, source in ((cst[:, C_LATER:], consts[:, C_LATER:]), (lam_q[:], lam_in), (subln[:], subln_in),
                                 (wf[:], wf_in), (bf[:], bf_in)):
                sp.dma_start(tile, source).then_inc(const_loaded, 16)
            rounds = CHUNKS // RAW - PEELED
            with sp.Fori(0, rounds) as turn:
                for k in range(RAW):
                    sp.wait_ge(lo_ready, turn * RAW + ((PEELED - 1) * RAW + k + 1))
                    load(RAW + k, turn * RAW + (PEELED * RAW + k))
            for c in range((rounds + PEELED) * RAW, CHUNKS):
                sp.wait_ge(lo_ready, c - RAW + 1)
                load(c, c)
            for d in range(DT):
                sp.wait_ge(y_ready, d + 1)
                sp.dma_start(out[:, d, :], x[:, d, :]).then_inc(stored, 16)
            sp.wait_ge(stored, 16 * DT)

        @block.gpsimd
        def _(pool):
            nc.gpsimd.memset(half_neg[:], -0.5).then_inc(const_ready, 1)
            pool.wait_ge(const_ready, 1)
            for n in range(NORMS):
                pool.wait_ge(mean_ready, n + 1)
                nc.gpsimd.tensor_tensor(r_col[:], mean[:], half_neg[:], ALU.pow).then_inc(r_col_ready, 1)

        @block.scalar
        def _(act):
            split = [0]
            own = [0]

            def own_step():
                own[0] += 1
                act.wait_ge(act_step, own[0])

            def hi(c, turn=0):
                act.wait_ge(raw_loaded[c % RAW], 16 * (c // RAW + 1) + turn * (16 * RING // RAW))
                slot_free(act, c, turn)
                nc.scalar.activation(w_hi[:, c % RING, :], raw[:, c % RAW, :], ACT.Copy).then_inc(hi_ready, 1)

            def first_hi(half):
                if half == 0:
                    act.wait_ge(raw_half_loaded, 16)
                    nc.scalar.activation(w_hi[:, 0, 0:HALF], raw[:, 0, 0:HALF], ACT.Copy).then_inc(hi_half_ready, 1)
                else:
                    act.wait_ge(raw_loaded[0], 16)
                    nc.scalar.activation(w_hi[:, 0, HALF:], raw[:, 0, HALF:], ACT.Copy).then_inc(hi_ready, 1)
                    split[0] = 1

            def split_to(c):
                while split[0] <= min(c, CHUNKS - 1):
                    hi(split[0])
                    split[0] += 1

            def ffn(layer, n, c0, _, f):
                split_to(c0 + 4)

                def step(s, c, turn):
                    t0 = f * FFN_TILES + 2 * s

                    def split_next(k):
                        if 2 <= s < UNITS - 1:
                            hi(c + 3 + k, turn)
                        elif s:
                            split_to(c + 3 + k)
                        else:
                            split_to(c + (6 if k == 3 else 5))

                    for k in range(2):
                        t = t0 + k
                        if k == 0 or s < UNITS - 1:
                            split_next(k)
                        act.wait_ge(gu_scaled, t + 1 + turn * 4)
                        nc.scalar.activation(silu_sb[t % 2], gu_sb[t % 2][:, 0, :], ACT.Silu).then_inc(silu_ready, 1)
                        if k == 1 and s < UNITS - 1:
                            split_next(2)
                        act.wait_ge(h_ready, t + 1 + turn * 4)
                        if k == 0 and s >= 2:
                            act.wait_ge(down_used, f * (UNITS - 1) + s - 1 + turn * 2)
                        nc.scalar.activation(m_hi[:, t % 4, :], h_sb[t % 2], ACT.Copy).then_inc(h_hi_ready, 1)
                        if s == 0 and k == 1:
                            split_next(3)

                for turns, body in ffn_steps(step, c0):
                    with act.Fori(0, turns) as turn:
                        body(turn)
                    split[0] = c0 + 3 * (UNITS - 2) - 1 + RING
                split_to(c0 + FFN_CHUNKS + 2)

            def attention(layer, n, c0, _, kind):
                first = layer * PAIRS
                kind = KINDS[layer]

                def values(j):
                    split_to(c0 + ATT_ORDER.index(("v", j)) + 3)
                    act.wait_ge(v_psum, first + j + 1)
                    if j == 0:
                        act.wait_ge(r_col_ready, n + 1)
                    for tb in range(TB):
                        ins = nc.scalar.activation(v[:, tb, j * COLS:(j + 1) * COLS],
                                                   work[:, V_BANK[j], tb * T:(tb + 1) * T],
                                                   ACT.Identity, scale=r_col[:, tb:tb + 1])
                    ins.then_inc(v_ready, 1)

                values(0)
                values(1)
                if layer == 0:
                    act.wait_ge(lam_psum, 1)
                    nc.scalar.activation(lam_e[:], work[:, 3, 0:2], ACT.Exp).then_inc(lam_exp, 1)
                if kind == FOX:
                    act.wait_ge(f_ready, 1)
                    nc.scalar.activation(fg[:, 1], fg[:, 0], ACT.Abs).then_inc(act_step, 1)
                    own_step()
                    nc.scalar.activation(fg[:, 1], fg[:, 1], ACT.Exp, scale=-1.0).then_inc(act_step, 1)
                    own_step()
                    nc.scalar.activation(fg[:, 2], fg[:, 1], ACT.Ln, bias=1.0).then_inc(f_ln, 1)
                values(2)
                values(3)

                def weights(b):
                    if kind == STICK:
                        act.wait_ge(logw_ready, KINDS[:layer].count(STICK) * PAIRS + b - first + 1)
                        nc.scalar.activation(w_t[:], s_b, ACT.Exp).then_inc(w_ready, 1)
                    else:
                        maps = 1 if kind == DIFF else 2
                        act.wait_ge(mixed_psum, b + 1)
                        nc.scalar.activation(w_t[:, 0:maps], attn[:, 0:maps], ACT.Copy).then_inc(w_ready, 1)

                def mix(b):
                    act.wait_ge(pv_psum, b + 1)
                    slot = 2 * (b % 2)
                    if kind != DIFF:
                        nc.scalar.activation(m_hi[:, slot:slot + 2, :], halves(work[:, 0, :]),
                                             ACT.Copy).then_inc(mix_hi_ready, 1)
                        return
                    nc.scalar.activation(head_out, work[:, 0, :], ACT.Copy)
                    nc.scalar.activation(scratch[:, 2, 0:2 * T], work[:, 0, :], ACT.Square).then_inc(osq_ready, 1)

                def sub_norm(b):
                    act.wait_ge(ovar_ready, b - first + 1)
                    nc.scalar.activation(scratch[:, 2, 0:T], scratch[:, 2, 0:T], ACT.Ln).then_inc(act_step, 1)
                    own_step()
                    nc.scalar.activation(scratch[:, 2, 0:T], scratch[:, 2, 0:T], ACT.Exp,
                                         scale=-0.5).then_inc(or_ready, 1)

                def sub_norm_split(b):
                    slot = 2 * (b % 2)
                    act.wait_ge(on_ready, b - first + 1)
                    for h in range(2):
                        ins = nc.scalar.activation(m_hi[:, slot + h, :], head_out[:, h * T:(h + 1) * T],
                                                   ACT.Identity, scale=subln_s[:, h:h + 1])
                    ins.then_inc(mix_hi_ready, 1)

                def exponentials(a):
                    act.wait_ge(scores_ready, a + 1)
                    if kind == STICK:
                        nc.scalar.activation(s_b, s_a, ACT.Abs).then_inc(act_step, 1)
                        own_step()
                        nc.scalar.activation(s_b, s_b, ACT.Exp, scale=-1.0).then_inc(act_step, 1)
                        own_step()
                        nc.scalar.activation(s_c, s_b, ACT.Ln, bias=1.0).then_inc(exp_ready, 1)
                    else:
                        for h in range(2):
                            for tb, cols in enumerate(ROWS):
                                ins = nc.scalar.activation(s_b[:, h, cols], s_a[:, h, cols], ACT.Exp,
                                                           bias=neg_max[:, h, tb:tb + 1],
                                                           accum_out=row_sum[:, h, tb:tb + 1])
                        ins.then_inc(exp_ready, 1)

                for j in range(PAIRS + 1):
                    a, b = first + j, first + j - 1
                    if j < PAIRS:
                        q_chunk = c0 + ATT_ORDER.index(("q", j))
                        split_to(q_chunk + 4)
                    if j:
                        weights(b)
                    if j < PAIRS:
                        split_to(q_chunk + (5 if j else 6))
                    if j:
                        mix(b)
                    if j and kind == DIFF:
                        sub_norm(b)
                    if j and kind == DIFF:
                        sub_norm_split(b)
                    if j < PAIRS:
                        exponentials(a)
                split_to(c0 + ATT_CHUNKS + 2)

            def square(d):
                nc.scalar.activation(squares[:, d:d + 2, :], x[:, d:d + 2, :], ACT.Square).then_inc(squares_ready, 1)

            def gains_and_squares(n):
                for d in range(DT):
                    if n:
                        act.wait_ge(x_updated, DT * (n - 1) + d + 1)
                    elif d % (DT // 2) == 0:
                        act.wait_ge(x_loaded[2 * d // DT], 16)
                    if n < NORMS - 1:
                        nc.scalar.activation(xg_hi[:, d, :], x[:, d, :], ACT.Identity,
                                             scale=gain[:, n, d:d + 1]).then_inc(xg_hi_ready, 1)
                    if n == 0 and d % (DT // 2) == DT // 2 - 1:
                        first_hi(2 * d // DT)
                    if d % 2 and n:
                        square(d - 1)
                if n == 0:
                    split_to(1)
                    for d in range(0, DT, 2):
                        square(d)

            act.wait_ge(gain_loaded, 16)
            nc.scalar.activation(warm[:], gain[:, 0, 0:1], ACT.Copy)
            gains_and_squares(0)
            for phase in phases():
                (attention if phase[3] else ffn)(*phase)
                gains_and_squares(phase[1] + 1)

        @block.vector
        def _(dve):
            split = [0]
            own = [0]

            def done(ins):
                own[0] += 1
                ins.then_inc(dve_step, 1)
                dve.wait_ge(dve_step, own[0])

            def lo(c, turn=0):
                dve.wait_ge(hi_ready, c + 1 + turn * RING)
                nc.vector.tensor_tensor(w_lo[:, c % RING, :], raw[:, c % RAW, :], w_hi[:, c % RING, :].bitcast(F32),
                                        ALU.subtract).then_inc(lo_ready, 1)

            def first_lo(half):
                if half == 0:
                    dve.wait_ge(hi_half_ready, 1)
                    nc.vector.tensor_tensor(w_lo[:, 0, 0:HALF], raw[:, 0, 0:HALF], w_hi[:, 0, 0:HALF].bitcast(F32),
                                            ALU.subtract).then_inc(lo_half_ready, 1)
                else:
                    dve.wait_ge(hi_ready, 1)
                    nc.vector.tensor_tensor(w_lo[:, 0, HALF:], raw[:, 0, HALF:], w_hi[:, 0, HALF:].bitcast(F32),
                                            ALU.subtract).then_inc(lo_ready, 1)
                    split[0] = 1

            def split_to(c):
                while split[0] <= min(c, CHUNKS - 1):
                    lo(split[0])
                    split[0] += 1

            def norm_mean(n):
                dve.wait_ge(var_ready, n + 1)
                nc.vector.tensor_scalar(mean[:], acc[:, 0, 0:TB], 1.0 / D, EPS, ALU.mult,
                                        ALU.add).then_inc(mean_ready, 1)

            def norm_diag(n):
                if n == 0:
                    dve.wait_ge(ones_loaded, 16)
                dve.wait_ge(r_col_ready, n + 1)
                for tb in range(TB):
                    ins = nc.vector.tensor_scalar(r_diag[:, tb * P:(tb + 1) * P], ident, r_col[:, tb:tb + 1], None,
                                                  ALU.mult)
                ins.then_inc(r_diag_ready, 1)

            def norm_row(n):
                dve.wait_ge(r_row_psum, n + 1)
                nc.vector.tensor_copy(r_row[:], acc[:, 1, 0:T]).then_inc(r_row_ready, 1)

            def ffn(layer, n, c0, _, f):
                split_to(c0 + 2)
                norm_mean(n)
                norm_diag(n)
                split_to(c0 + 3)
                norm_row(n)
                dve.wait_ge(r_row_ready, n + 1)

                def step(s, c, turn):
                    t0 = f * FFN_TILES + 2 * s

                    def split_next(k):
                        if 2 <= s < UNITS - 1:
                            lo(c + 3 + k, turn)
                        elif s:
                            split_to(c + 3 + k)
                        else:
                            split_to(c + (6 if k == 3 else 4))

                    for k in range(2):
                        t = t0 + k
                        dve.wait_ge(gu_psum, t + 1 + turn * 4)
                        nc.vector.tensor_tensor(gu_sb[t % 2], halves(work[:, t % 4, :]), both(r_row[:]),
                                                ALU.mult).then_inc(gu_scaled, 1)
                        if k == 0 or s < UNITS - 1:
                            split_next(2 * k)
                        dve.wait_ge(silu_ready, t + 1 + turn * 4)
                        nc.vector.tensor_tensor(h_sb[t % 2], silu_sb[t % 2], gu_sb[t % 2][:, 1, :],
                                                ALU.mult).then_inc(h_ready, 1)
                        if k == 0 and 0 < s < UNITS - 1:
                            split_next(1)
                        dve.wait_ge(h_hi_ready, t + 1 + turn * 4)
                        nc.vector.tensor_tensor(m_lo[:, t % 4, :], h_sb[t % 2], m_hi[:, t % 4, :].bitcast(F32),
                                                ALU.subtract).then_inc(h_split, 1)
                        if s == 0 and k == 1:
                            split_next(3)

                for turns, body in ffn_steps(step, c0):
                    with dve.Fori(0, turns) as turn:
                        body(turn)
                    split[0] = c0 + 3 * (UNITS - 2) - 1 + RING
                split_to(c0 + FFN_CHUNKS + 1)

            def attention(layer, n, c0, _, kind):
                kind = KINDS[layer]
                first = layer * PAIRS
                if layer == 0:
                    dve.wait_ge(const_loaded, 16 * 5)
                split_to(c0 + 2)
                norm_mean(n)
                norm_diag(n)
                split_to(c0 + 3)
                norm_row(n)
                split_to(c0 + 4)
                if layer == 0:
                    lp = lam_q[:].rearrange("p (a b) -> p a b", b=2)
                    nc.vector.tensor_tensor(lam_p[:], lp[:, :, 0], lp[:, :, 1], ALU.mult).then_inc(lam_in_ready, 1)
                if kind == DIFF:
                    nc.vector.tensor_scalar(subln_s[:], subln[:], 1.0 - LAM_INIT, None, ALU.mult)
                    dve.wait_ge(lam_exp, 1)
                    done(nc.vector.tensor_tensor(lam[:, 0:1], lam_e[:, 0:1], lam_e[:, 1:2], ALU.subtract))
                    done(nc.vector.tensor_scalar(lam[:, 1:2], lam[:, 0:1], LAM_INIT, None, ALU.add))
                if kind == FOX:
                    dve.wait_ge(f_psum, 1)
                    for tb in range(TB):
                        ins = nc.vector.scalar_tensor_tensor(
                            out=fg[:, 0, tb, :], in0=work[:, 3, tb * 8:(tb + 1) * 8], scalar=r_col[:, tb:tb + 1],
                            in1=bf[:], op0=ALU.mult, op1=ALU.add)
                    ins.then_inc(f_ready, 1)
                    dve.wait_ge(f_ln, 1)
                    nc.vector.scalar_tensor_tensor(out=flat(fg[:, 3]), in0=flat(fg[:, 0]), scalar=0.0,
                                                   in1=flat(fg[:, 2]), op0=ALU.min,
                                                   op1=ALU.subtract).then_inc(logf_ready, 1)
                dve.wait_ge(r_row_ready, n + 1)

                def forget_cums():
                    dve.wait_ge(cum_psum, 1)
                    nc.vector.tensor_copy(flat(cum_col[:]), work[:, 3, 0:2 * 8])
                    for head in range(2 * PAIRS):
                        for tb in range(TB):
                            ins = nc.vector.tensor_scalar(lf_wide[:, head, tb, :], ones, fg[:, 3, tb, head:head + 1],
                                                          None, ALU.mult)
                    ins.then_inc(lf_wide_ready, 1)

                def forget_bias():
                    for pair in range(PAIRS):
                        dve.wait_ge(bias_psum, pair + 1)
                        for h in range(2):
                            bank = work[:, 1 if pair % 2 else 3, h * T:(h + 1) * T]
                            head = 2 * pair + h
                            nc.vector.tensor_tensor(wide[:, head, 0:P], causal[:, 0:P], bank[:, 0:P], ALU.subtract)
                            ins = nc.vector.tensor_tensor(wide[:, head, P:TRI], causal[:, P:TRI], bank, ALU.subtract)
                        ins.then_inc(bias_ready, 1)
                    dve.wait_ge(bias_ready, PAIRS)

                def scale_qk(dst, bank, count, scale):
                    dve.wait_ge(qk_psum, count)
                    nc.vector.scalar_tensor_tensor(out=dst[:], in0=halves(work[:, bank, :]), scalar=scale,
                                                   in1=both(r_row[:]), op0=ALU.mult,
                                                   op1=ALU.mult).then_inc(rope_in if kind == DIFF else qk_ready, 1)

                def rotate(dst, bank, k):
                    turned = wide[0:ROT, 0:2, 0:T]
                    dve.wait_ge(rope_psum, k)
                    nc.vector.tensor_tensor(dst[0:ROT], dst[0:ROT], both(cos), ALU.mult)
                    done(nc.vector.tensor_tensor(turned, halves(work[0:ROT, bank, :]), both(sin), ALU.mult))
                    nc.vector.tensor_tensor(dst[0:ROT], dst[0:ROT], turned, ALU.add).then_inc(qk_ready, 1)

                def log_weights(b):
                    dve.wait_ge(mixed_psum, b + 1)
                    nc.vector.tensor_tensor(s_b, s_a, attn, ALU.subtract).then_inc(logw_ready, 1)

                def mix(b):
                    slot = 2 * (b % 2)
                    dve.wait_ge(mix_hi_ready, b + 1)
                    nc.vector.tensor_tensor(m_lo[:, slot:slot + 2, :], halves(work[:, 0, :]),
                                            m_hi[:, slot:slot + 2, :].bitcast(F32),
                                            ALU.subtract).then_inc(mix_ready, 1)

                def sub_norm_mean(b):
                    dve.wait_ge(ovar_psum, b - first + 1)
                    nc.vector.tensor_scalar(scratch[:, 2, 0:T], work[:, 3, 0:T], 1.0 / COLS, EPS, ALU.mult,
                                            ALU.add).then_inc(ovar_ready, 1)

                def sub_norm(b):
                    dve.wait_ge(or_ready, b - first + 1)
                    nc.vector.tensor_tensor(halves(head_out), halves(head_out), both(scratch[:, 2, 0:T]),
                                            ALU.mult).then_inc(on_ready, 1)

                def sub_norm_split(b):
                    slot = 2 * (b % 2)
                    dve.wait_ge(mix_hi_ready, b + 1)
                    for h in range(2):
                        ins = nc.vector.scalar_tensor_tensor(
                            out=m_lo[:, slot + h, :], in0=head_out[:, h * T:(h + 1) * T],
                            scalar=subln_s[:, h:h + 1], in1=m_hi[:, slot + h, :].bitcast(F32),
                            op0=ALU.mult, op1=ALU.subtract)
                    ins.then_inc(mix_ready, 1)

                def mask(a):
                    j = a - first
                    dve.wait_ge(scores_psum, a + 1)
                    if kind == STICK:
                        nc.vector.tensor_tensor(s_a, attn, both(strict_t), ALU.add).then_inc(scores_ready, 1)
                        return
                    if kind == DIFF:
                        done(nc.vector.tensor_tensor(s_a, attn, both(causal), ALU.add))
                    else:
                        for h in range(2):
                            for tb, cols in enumerate(ROWS):
                                ins = nc.vector.scalar_tensor_tensor(
                                    out=s_a[:, h, cols], in0=attn[:, h, cols],
                                    scalar=cum_col[:, tb, 2 * j + h:2 * j + h + 1],
                                    in1=wide[:, 2 * j + h, cols], op0=ALU.add, op1=ALU.add)
                        done(ins)
                    for tb, cols in enumerate(ROWS):
                        ins = nc.vector.tensor_reduce(row_max[:, :, tb], s_a[:, :, cols], AX_X, ALU.max)
                    done(ins)
                    nc.vector.tensor_scalar(neg_max[:], row_max[:], -1.0, None, ALU.mult).then_inc(scores_ready, 1)

                def normalise(a):
                    dve.wait_ge(exp_ready, a + 1)
                    if kind == STICK:
                        nc.vector.scalar_tensor_tensor(out=s_c, in0=s_a, scalar=0.0, in1=s_c, op0=ALU.max,
                                                       op1=ALU.add).then_inc(mix_in, 1)
                        return
                    done(nc.vector.reciprocal(row_inv[:], row_sum[:]))
                    if kind == FOX:
                        for h in range(2):
                            for tb, cols in enumerate(ROWS):
                                ins = nc.vector.tensor_scalar(s_a[:, h, cols], s_b[:, h, cols],
                                                              row_inv[:, h, tb:tb + 1], None, ALU.mult)
                        ins.then_inc(mix_in, 1)
                        return
                    for tb, cols in enumerate(ROWS):
                        ins = nc.vector.tensor_scalar(s_a[:, 1, cols], s_b[:, 1, cols], row_inv[:, 1, tb:tb + 1],
                                                      lam[:, 1:2], ALU.mult, ALU.mult)
                    done(ins)
                    for tb, cols in enumerate(ROWS):
                        ins = nc.vector.scalar_tensor_tensor(
                            out=s_a[:, 0, cols], in0=s_b[:, 0, cols], scalar=row_inv[:, 0, tb:tb + 1],
                            in1=s_a[:, 1, cols], op0=ALU.mult, op1=ALU.subtract)
                    ins.then_inc(mix_in, 1)

                for j in range(PAIRS + 1):
                    a, b = first + j, first + j - 1
                    if j < PAIRS:
                        q_chunk = c0 + ATT_ORDER.index(("q", j))
                        if kind != DIFF or j == 0:
                            split_to(q_chunk + 3)
                        if not (kind == DIFF and j == 2):
                            scale_qk(q_t, 0, 2 * a + 1, SCALE)
                        split_to(q_chunk + 3)
                        if kind == FOX and j == 0:
                            forget_cums()
                        if kind == DIFF:
                            rotate(q_t, 0, 2 * j + 1)
                        if kind == STICK and j in (1, 3):
                            log_weights(b)
                        if kind == STICK or kind == DIFF and j < 2 or kind == FOX and j != 1:
                            split_to(q_chunk + 4)
                    if kind == STICK and j in (2, 4):
                        log_weights(b)
                    if j < PAIRS:
                        scale_qk(k_t, 1, 2 * a + 2, 1.0)
                        if kind == FOX and j == 1:
                            split_to(q_chunk + 4)
                        if kind == DIFF:
                            rotate(k_t, 1, 2 * j + 2)
                        if kind == FOX and j == 0:
                            forget_bias()
                    if j and kind != DIFF:
                        mix(b)
                    if j and kind == DIFF:
                        sub_norm_mean(b)
                        if j < PAIRS:
                            split_to(q_chunk + (5 if j == 1 else 4))
                        sub_norm(b)
                        if j == 2:
                            split_to(q_chunk + 5)
                    if j < PAIRS:
                        if j == 0:
                            split_to(q_chunk + 5)
                        mask(a)
                        if j and kind == DIFF:
                            sub_norm_split(b)
                        elif kind != DIFF or j == 0:
                            split_to(q_chunk + (5 if j else 6))
                        if kind == DIFF and j == 1:
                            scale_qk(q_t, 0, 2 * a + 3, SCALE)
                        normalise(a)
                        split_to(q_chunk + 5)
                    elif kind == DIFF:
                        sub_norm_split(b)
                split_to(c0 + ATT_CHUNKS + 1)

            def add_squares(n, i):
                dve.wait_ge(squares_ready, n * (DT // 2) + i + 1)
                done(nc.vector.tensor_tensor(squares[:, 0:2, :], squares[:, 0:2, :], squares[:, 2 * i:2 * i + 2, :],
                                             ALU.add))

            def update(n, scale):
                for d in range(DT + 1):
                    if n == 0 and d % (DT // 2) == 1:
                        dve.wait_ge(x_loaded[2 * d // DT], 16)
                    if d < DT and n:
                        if d % 2 == 0:
                            dve.wait_ge(acc_ready, DT * (n - 1) + d + 2)
                        nc.vector.scalar_tensor_tensor(out=x[:, d, :], in0=acc_tile(d), scalar=scale, in1=x[:, d, :],
                                                       op0=ALU.mult, op1=ALU.add).then_inc(x_updated, 1)
                    if d and n < NORMS - 1:
                        dve.wait_ge(xg_hi_ready, DT * n + d)
                        nc.vector.scalar_tensor_tensor(
                            out=xg_lo[:, d - 1, :], in0=x[:, d - 1, :], scalar=gain[:, n, d - 1:d],
                            in1=xg_hi[:, d - 1, :].bitcast(F32), op0=ALU.mult, op1=ALU.subtract).then_inc(xg_ready, 1)
                    if n == 0 and d and d % (DT // 2) == 0:
                        first_lo(2 * d // DT - 1)
                    if 0 < n < NORMS - 1 and (d in (5, 7) or d == DT):
                        add_squares(n, (d - 3) // 2 if d < DT else 3)
                if n == 0:
                    split_to(1)
                    for i in range(1, DT // 2):
                        add_squares(n, i)
                if n < NORMS - 1:
                    nc.vector.tensor_tensor(squares[:, 0, :], squares[:, 0, :], squares[:, 1, :],
                                            ALU.add).then_inc(square_sum_ready, 1)

            dve.wait_ge(gain_loaded, 16)
            update(0, 1.0)
            for phase in phases():
                (attention if phase[3] else ffn)(*phase)
                update(phase[1] + 1, 1.0 if phase[3] else 0.5)

            n = NORMS - 1
            norm_mean(n)
            norm_diag(n)
            dve.wait_ge(r_row_psum, n + 1)
            for d in range(DT):
                nc.vector.scalar_tensor_tensor(out=x[:, d, :], in0=x[:, d, :], scalar=gain[:, n, d:d + 1],
                                               in1=acc[:, 1, 0:T], op0=ALU.mult,
                                               op1=ALU.mult).then_inc(y_ready, 1)

        @block.tensor
        def _(pe):
            def product(dst, a_hi, a_lo, b_hi, b_lo, start, stop, skip=False):
                nc.tensor.matmul(dst, a_hi, b_hi, start=start, stop=False, skip_group_check=skip)
                nc.tensor.matmul(dst, a_hi, b_lo, start=False, stop=False, skip_group_check=skip)
                return nc.tensor.matmul(dst, a_lo, b_hi, start=False, stop=stop, skip_group_check=skip)

            def project(dst, c, col, row_of=None):
                for k in range(DT):
                    if row_of is not None and k == DT // 2:
                        norm_row(row_of)
                    ins = product(dst, proj(w_hi, c)[:, k, col:col + P], proj(w_lo, c)[:, k, col:col + P],
                                  xg_hi[:, k, :], xg_lo[:, k, :], start=k == 0, stop=k == DT - 1)
                return ins

            def contract_pair(c, slot, first, last, banks=(0, 1, 2, 3)):
                for d, t in [(d, t) for bank in (2 * i for i in banks) for t in range(2) for d in (bank, bank + 1)]:
                    ins = product(acc_tile(d), down(w_hi, c)[:, t, d * P:(d + 1) * P],
                                  down(w_lo, c)[:, t, d * P:(d + 1) * P], m_hi[:, slot + t, :], m_lo[:, slot + t, :],
                                  start=first and t == 0 and d % 2 == 0, stop=last and t == 1, skip=True)
                    if last and t == 1:
                        ins.then_inc(acc_ready, 1)
                return ins

            def norm_var(n):
                if n == 0:
                    pe.wait_ge(ones_loaded, 16)
                pe.wait_ge(square_sum_ready, n + 1)
                for tb in range(TB):
                    ins = nc.tensor.matmul(acc[:, 0, tb:tb + 1], squares[:, 0, tb * P:(tb + 1) * P], ones[:, 0:1],
                                           start=True, stop=True)
                ins.then_inc(var_ready, 1)

            def last_norm_var():
                pe.wait_ge(x_updated, DT * (NORMS - 1))
                for i in range(DT // 2):
                    pe.wait_ge(squares_ready, (NORMS - 1) * (DT // 2) + i + 1)
                    for d in (2 * i, 2 * i + 1):
                        for tb in range(TB):
                            ins = nc.tensor.matmul(acc[:, 0, tb:tb + 1], squares[:, d, tb * P:(tb + 1) * P],
                                                   ones[:, 0:1], start=d == 0 and tb == 0, stop=d == DT - 1,
                                                   skip_group_check=True)
                ins.then_inc(var_ready, 1)

            def norm_row(n):
                pe.wait_ge(r_diag_ready, n + 1)
                nc.tensor.matmul(acc[:, 1, 0:T], ones, r_diag[:], start=True, stop=True).then_inc(r_row_psum, 1)

            def ffn(layer, n, c0, _, f):
                def first_step():
                    for parts in (((0,), (1,)) if n == 0 else ((0, 1),)):
                        if n == 0 and parts[0] == 0:
                            pe.wait_ge(lo_half_ready, 1)
                        else:
                            pe.wait_ge(lo_ready, c0 + parts[-1] + 1)
                        for k in range(DT):
                            if n == 0 and parts[0] == 0 and k == DT // 2:
                                pe.wait_ge(lo_ready, 1)
                            if parts[0] == 0:
                                pe.wait_ge(xg_ready, DT * n + k + 1)
                            for part in parts:
                                for i in range(2):
                                    t = f * FFN_TILES + i
                                    ins = product(work[:, t % 4, part * T:(part + 1) * T],
                                                  proj(w_hi, c0 + part)[:, k, i * P:(i + 1) * P],
                                                  proj(w_lo, c0 + part)[:, k, i * P:(i + 1) * P],
                                                  xg_hi[:, k, :], xg_lo[:, k, :],
                                                  start=k == 0 and part == 0, stop=k == DT - 1, skip=True)
                                    if k == DT - 1 and part:
                                        ins.then_inc(gu_psum, 1)
                                    elif k == DT - 1 and i:
                                        ins.then_inc(gate_used, 1)
                            if k == NORM_AT and parts[-1] == 1:
                                norm_var(n)

                def step(s, c, turn):
                    if s == 0:
                        first_step()
                        return
                    for k in range(2):
                        t = f * FFN_TILES + 2 * s + k
                        if s >= 2:
                            pe.wait_ge(gu_scaled, t - 3 + turn * 4)
                        if k == 0:
                            pe.wait_ge(lo_ready, c + 1 + turn * RING)
                        ins = project(work[:, t % 4, 0:T], c, k * P, row_of=n if s == 1 and k == 0 else None)
                        if k == 1:
                            ins.then_inc(gate_used, 1)
                        else:
                            pe.wait_ge(lo_ready, c + 2 + turn * RING)
                        project(work[:, t % 4, T:2 * T], c + 1, k * P).then_inc(gu_psum, 1)
                    unit_down(s - 1, c + 2, turn).then_inc(down_used, 1)

                def unit_down(u, c, turn, last=False):
                    pe.wait_ge(lo_ready, c + 1 + turn * RING)
                    pe.wait_ge(h_split, f * FFN_TILES + 2 * u + 2 + turn * 4)
                    return contract_pair(c, (f * FFN_TILES + 2 * u) % 4, u == 0, last)

                for turns, body in ffn_steps(step, c0):
                    with pe.Fori(0, turns) as turn:
                        body(turn)
                unit_down(UNITS - 1, c0 + FFN_CHUNKS - 1, 0, True)

            def attention(layer, n, c0, _, kind):
                kind = KINDS[layer]
                first = layer * PAIRS
                if layer == 0:
                    pe.wait_ge(const_loaded, 16 * 5)

                def values(js):
                    pe.wait_ge(lo_ready, c0 + ATT_ORDER.index(("v", js[-1])) + 1)
                    for k in range(DT):
                        if js[0] == 0:
                            pe.wait_ge(xg_ready, DT * n + k + 1)
                        for j in js:
                            c = c0 + ATT_ORDER.index(("v", j))
                            for tb in range(TB):
                                ins = product(work[:, V_BANK[j], tb * T:(tb + 1) * T],
                                              xg_hi[:, k, tb * P:(tb + 1) * P], xg_lo[:, k, tb * P:(tb + 1) * P],
                                              proj(w_hi, c)[:, k, :], proj(w_lo, c)[:, k, :],
                                              start=k == 0 and tb == 0, stop=k == DT - 1, skip=True)
                            if k == DT - 1:
                                ins.then_inc(v_psum, 1)
                        if js[0] == 0 and k == NORM_AT:
                            norm_var(n)

                def lambda_sums():
                    pe.wait_ge(lam_in_ready, 1)
                    nc.tensor.matmul(work[:, 3, 0:2], ones, lam_p[:], start=True, stop=True).then_inc(lam_psum, 1)

                def forget_logits():
                    for tb in range(TB):
                        for k in range(DT):
                            for part in (xg_hi, xg_lo):
                                ins = nc.tensor.matmul(
                                    work[:, 3, tb * 8:(tb + 1) * 8], part[:, k, tb * P:(tb + 1) * P].bitcast(F32),
                                    wf[:, k, :], start=k == 0 and part is xg_hi, stop=k == DT - 1 and part is xg_lo)
                    ins.then_inc(f_psum, 1)

                def head_projection(c, bank, h):
                    pe.wait_ge(lo_ready, c + 1)
                    ins = project(work[:, bank, h * T:(h + 1) * T], c, h * P)
                    if h:
                        ins.then_inc(qk_psum, 1)

                def rotate(t, bank, j, k):
                    pe.wait_ge(rope_in, 2 * j + k)
                    nc.tensor.matmul(work[0:ROT, bank, :], rot, flat(t[0:ROT]), start=True,
                                     stop=True).then_inc(rope_psum, 1)

                def forget_cums():
                    pe.wait_ge(logf_ready, 1)
                    nc.tensor.matmul(work[:, 3, 0:8], cum[:, 0:P], fg[:, 3, 0, :], start=True, stop=True)
                    nc.tensor.matmul(work[:, 3, 8:16], ones, fg[:, 3, 0, :], start=True, stop=False)
                    nc.tensor.matmul(work[:, 3, 8:16], cum[:, 0:P], fg[:, 3, 1, :], start=False,
                                     stop=True).then_inc(cum_psum, 1)

                def forget_bias(pairs):
                    pe.wait_ge(lf_wide_ready, 1)
                    for pair in pairs:
                        if pair == 1:
                            pe.wait_ge(qk_ready, 2 * first + 2)
                        if pair >= 2:
                            pe.wait_ge(bias_ready, pair - 1)
                        for h in range(2):
                            bank, head = work[:, 1 if pair % 2 else 3, h * T:(h + 1) * T], 2 * pair + h
                            nc.tensor.matmul(bank, lf_wide[:, head, 0, :], cum, start=True, stop=True)
                            ins = nc.tensor.matmul(bank[:, P:T], lf_wide[:, head, 1, :], cum[:, 0:P], start=False,
                                                   stop=True, skip_group_check=True)
                        ins.then_inc(bias_psum, 1)

                def scores(a):
                    pe.wait_ge(qk_ready, 2 * a + 2)
                    for h in range(2):
                        if kind == DIFF and h and a > first:
                            pe.wait_ge(ovar_ready, a - first)
                        q, k, bank = q_t[:, h, :], k_t[:, h, :], work[:, 2 + h, :]
                        if kind == STICK:
                            nc.tensor.matmul(bank[:, 0:T], k[:, 0:P], q, start=True, stop=True)
                            ins = nc.tensor.matmul(bank[:, T:TRI], k[:, P:T], q[:, P:T], start=True, stop=True)
                        else:
                            nc.tensor.matmul(bank[:, 0:P], q[:, 0:P], k[:, 0:P], start=True, stop=True)
                            ins = nc.tensor.matmul(bank[:, P:TRI], q[:, P:T], k, start=True, stop=True)
                    ins.then_inc(scores_psum, 1)

                def mixed(b):
                    pe.wait_ge(mix_in, b + 1)
                    for h in range(1 if kind == DIFF else 2):
                        bank = work[:, 2 + h, :]
                        if kind == STICK:
                            nc.tensor.matmul(bank[:, 0:TRI], later, s_c[:, h, :], start=True, stop=True)
                            ins = nc.tensor.matmul(bank[:, P:T], ones, s_c[:, h, T:TRI], start=False, stop=True,
                                                   skip_group_check=True)
                        else:
                            for at in range(0, TRI, P):
                                ins = nc.tensor.transpose(bank[:, at:at + P], s_a[:, h, at:at + P], ident)
                    ins.then_inc(mixed_psum, 1)

                def weighted_values(b):
                    pe.wait_ge(w_ready, b + 1)
                    for h in range(2):
                        head = 2 * (b - first) + h
                        bank, cols = work[:, 0, h * T:(h + 1) * T], slice(head * HD, (head + 1) * HD)
                        w = w_t[:, 0 if kind == DIFF else h, :]
                        nc.tensor.matmul(bank, v[:, 0, cols], w[:, 0:T], start=True, stop=True)
                        ins = nc.tensor.matmul(bank[:, P:T], v[:, 1, cols], w[:, T:TRI], start=False, stop=True,
                                               skip_group_check=True)
                    ins.then_inc(pv_psum, 1)

                def output_squares(j):
                    pe.wait_ge(osq_ready, j)
                    nc.tensor.matmul(work[:, 3, 0:T], ones, scratch[:, 2, 0:T], start=True, stop=False)
                    nc.tensor.matmul(work[:, 3, 0:T], ones, scratch[:, 2, T:2 * T], start=False,
                                     stop=True).then_inc(ovar_psum, 1)

                def output(j, banks=(0, 1, 2, 3)):
                    c, b = c0 + ATT_ORDER.index(("o", j)), first + j
                    if banks[0] == 0:
                        pe.wait_ge(lo_ready, c + 1)
                        pe.wait_ge(mix_ready, b + 1)
                    ins = contract_pair(c, 2 * (b % 2), j == 0, j == PAIRS - 1, banks)
                    if banks[-1] == 3 and j < PAIRS - 1:
                        ins.then_inc(out_used, 1)

                values((0, 1))
                for j in range(PAIRS):
                    a, b = first + j, first + j - 1
                    c = c0 + ATT_ORDER.index(("q", j))
                    if j == 1:
                        pe.wait_ge(v_ready, first + PAIRS)
                    if j >= 2:
                        pe.wait_ge(osq_ready, j - 1) if kind == DIFF else pe.wait_ge(mix_ready, b)
                    if not (kind == DIFF and j == 2):
                        head_projection(c, 0, 0)
                    if j == 0:
                        pe.wait_ge(v_ready, first + 2)
                        if kind == FOX:
                            forget_logits()
                        norm_row(n)
                    head_projection(c, 0, 1)
                    if kind == FOX and j == 1:
                        pe.wait_ge(bias_ready, PAIRS)
                    head_projection(c + 1, 1, 0)
                    if j == 0 and kind == FOX:
                        forget_cums()
                    if j == 0 and layer == 0:
                        lambda_sums()
                    if kind == DIFF:
                        rotate(q_t, 0, j, 1)
                    if j:
                        mixed(b)
                    head_projection(c + 1, 1, 1)
                    if j == 0:
                        values((2,))
                        if kind == DIFF:
                            rotate(k_t, 1, j, 2)
                        if kind == FOX:
                            forget_bias((0, 1))
                        pe.wait_ge(qk_ready, 2 * a + 1)
                        values((3,))
                        if kind == FOX:
                            forget_bias((2, 3))
                            pe.wait_ge(bias_ready, 3)
                        if layer == 0:
                            pe.wait_ge(lam_exp, 1)
                        pe.wait_ge(v_ready, first + 3)
                        scores(a)
                        continue
                    pe.wait_ge(qk_ready, 2 * a + 1)
                    weighted_values(b)
                    if kind == DIFF:
                        rotate(k_t, 1, j, 2)
                    if kind == DIFF:
                        output_squares(j)
                    if kind == DIFF and j == 1:
                        head_projection(c0 + ATT_ORDER.index(("q", 2)), 0, 0)
                    if j == 2:
                        output(0)
                    if kind == DIFF and j == 3:
                        output(1, (0, 1))
                    scores(a)
                last = first + PAIRS - 1
                output(PAIRS - 3, (2, 3) if kind == DIFF else (0, 1, 2, 3))
                before, between = ((), (0, 1)) if kind == STICK else ((0,), (1,))
                if before:
                    output(PAIRS - 2, before)
                mixed(last)
                output(PAIRS - 2, between)
                weighted_values(last)
                if kind == DIFF:
                    output(PAIRS - 2, (2,))
                    output_squares(PAIRS)
                output(PAIRS - 2, (3,) if kind == DIFF else (2, 3))
                output(PAIRS - 1)

            for phase in phases():
                (attention if phase[3] else ffn)(*phase)
            last_norm_var()
            norm_row(NORMS - 1)


def kernel(x, norm_g, final_g, ffn_w_gate, ffn_w_up, ffn_w_down, w_qkv, w_o,
           diff_lambda, diff_subln_g, fox_w_f, fox_b_f):
    import concourse.bacc as bacc
    from concourse.bass_utils import run_bass_kernel_spmd

    a = [np.asarray(w) for w in (ffn_w_gate, ffn_w_up, ffn_w_down, w_qkv, w_o)]
    gate, up, down_w, qkv, w_out = a
    stream = np.empty((CHUNKS, P, CHUNK), np.float32)
    columns = lambda w, u: w[:, u * COLS:(u + 1) * COLS].reshape(DT, P, COLS).transpose(1, 0, 2).reshape(P, CHUNK)
    rows = lambda w, u: w[u * 2 * P:(u + 1) * 2 * P].reshape(2, P, D).transpose(1, 0, 2).reshape(P, CHUNK)
    chunks = []
    for layer in range(DEPTH):
        for part in range(3):
            if part == 1:
                w = qkv[layer]
                cut = {"q": w[:, :D], "k": w[:, D:2 * D], "v": w[:, 2 * D:]}
                chunks += [rows(w_out[layer], j) if what == "o" else columns(cut[what], j) for what, j in ATT_ORDER]
            else:
                cut = {"gate": gate[layer, part // 2], "up": up[layer, part // 2]}
                chunks += [rows(down_w[layer, part // 2], u) if what == "down" else columns(cut[what], u)
                           for what, u in FFN_ORDER]
    for c, chunk in enumerate(chunks):
        stream[c] = chunk
    tiles = lambda t: np.ascontiguousarray(np.asarray(t).reshape(DT, P, -1).transpose(1, 0, 2))
    gains = np.concatenate([np.asarray(norm_g).reshape(3 * DEPTH, D), np.asarray(final_g).reshape(1, D)])
    arrays = {
        "stream": stream,
        "x": tiles(np.asarray(x)[0].T),
        "gains": np.ascontiguousarray(gains.reshape(NORMS, DT, P).transpose(2, 0, 1)),
        "consts": constants(),
        "lam": np.ascontiguousarray(np.asarray(diff_lambda)[0].T),
        "subln": np.ascontiguousarray(np.asarray(diff_subln_g)[0].reshape(2, P).T),
        "wf": tiles(np.asarray(fox_w_f)[0]),
        "bf": np.ascontiguousarray(np.broadcast_to(np.asarray(fox_b_f)[0], (P, 8))),
    }
    nc = bacc.Bacc("TRN2", target_bir_lowering=False, num_devices=1)
    args = [nc.dram_tensor(f"{name}_dram", arr.shape, F32, kind="ExternalInput").ap() for name, arr in arrays.items()]
    out = nc.dram_tensor("out_dram", (P, DT, T), F32, kind="ExternalOutput").ap()
    trunk(nc, *args, out)
    ins = {f"{name}_dram": arr for name, arr in arrays.items()}
    y = run_bass_kernel_spmd(nc, [ins], core_ids=[0]).results[0]["out_dram"]
    return np.ascontiguousarray(y.transpose(2, 1, 0).reshape(1, T, D))
```
